# Optimizing a Trainium2 kernel written in Bass

```python
import math
import jax
import jax.numpy as jnp
from jax import lax
import numpy as np

D_MODEL = 2048
BATCH = 1
SEQ = 256
DEPTH = 1

GRID_W = 64
CTX_LEN = 256
EPS = 1e-6

HEAD_DIM = 128
N_Q_HEADS = 8
N_KV_HEADS = 2
Q_PER_KV = N_Q_HEADS // N_KV_HEADS
ATTN_WIDTH = N_Q_HEADS * HEAD_DIM
KV_WIDTH = N_KV_HEADS * HEAD_DIM
WINDOW = 128
ATTN_BLOCK = 128
ROPE_THETA = 10000.0
ROPE_PAIRS_PER_AXIS = HEAD_DIM // 4

HYENA_WIDTH = D_MODEL // 4
HYENA_ORDER = 2
HYENA_SHORT_W = 3
HYENA_BANDS = 16
HYENA_EMB = 1 + 2 * HYENA_BANDS
HYENA_FILTER_HIDDEN = 64
HYENA_DECAY_TARGET = 1e-2
HYENA_FAST_DECAY = 0.3
HYENA_SLOW_DECAY = 1.5

LRU_WIDTH = D_MODEL // 4
LRU_BLOCKS = 8
LRU_BLOCK = LRU_WIDTH // LRU_BLOCKS
LRU_CONV_W = 4
LRU_C = 8.0

N_BRANCH = 3
CTX_STATE_COLS = 2 * KV_WIDTH + LRU_WIDTH
Q_OFF = CTX_STATE_COLS
HY_OFF = Q_OFF + ATTN_WIDTH
LRU_Y_OFF = HY_OFF + 3 * HYENA_WIDTH
GATE_OFF = LRU_Y_OFF + LRU_WIDTH
D_IN = GATE_OFF + N_BRANCH * D_MODEL

N_EXPERTS = 16
N_GROUPS = 4
EXPERTS_PER_GROUP = N_EXPERTS // N_GROUPS
TOP_K = 2
D_EXPERT = D_MODEL // 4

kernel_name = 'hybrid_dit_hyena_swa_rglru_moe'

F32 = jnp.float32

def rmsnorm(x, g):
    xf = x.astype(F32)
    y = xf * lax.rsqrt(jnp.mean(xf * xf, axis=-1, keepdims=True) + EPS)
    return (y * g.astype(F32)).astype(x.dtype)

def modulate(x, shift, scale):
    return x * (1.0 + scale) + shift

def dwconv(u, w, b):
    width, ch = w.shape
    left = width // 2
    y = lax.conv_general_dilated(u, w[:, None, :].astype(u.dtype), window_strides=(1,),
                                 padding=[(left, width - 1 - left)],
                                 dimension_numbers=('NWC', 'WIO', 'NWC'),
                                 feature_group_count=ch)
    return y + b.astype(u.dtype)

def axial_rope_tables(n_tokens):
    rows = n_tokens // GRID_W
    row = jnp.repeat(jnp.arange(rows), GRID_W).astype(F32)
    col = jnp.tile(jnp.arange(GRID_W), rows).astype(F32)
    inv = ROPE_THETA ** (-jnp.arange(ROPE_PAIRS_PER_AXIS, dtype=F32) / ROPE_PAIRS_PER_AXIS)
    ang = jnp.concatenate([row[:, None] * inv, col[:, None] * inv], axis=-1)
    return jnp.cos(ang), jnp.sin(ang)

def apply_rope(x, cos, sin):
    xf = x.astype(F32)
    x1, x2 = xf[..., :HEAD_DIM // 2], xf[..., HEAD_DIM // 2:]
    c = cos[None, :, None, :]
    s = sin[None, :, None, :]
    return jnp.concatenate([x1 * c - x2 * s, x2 * c + x1 * s], axis=-1).astype(x.dtype)

def split_state(p):
    return p[..., :KV_WIDTH], p[..., KV_WIDTH:2 * KV_WIDTH], p[..., 2 * KV_WIDTH:CTX_STATE_COLS]

def split_rest(p):
    return p[..., Q_OFF:HY_OFF], p[..., HY_OFF:LRU_Y_OFF], p[..., LRU_Y_OFF:GATE_OFF], p[..., GATE_OFF:]

def sink_softmax(s, sink):
    s = s.astype(F32)
    sk = jnp.broadcast_to(sink.astype(F32), s.shape[:-1] + (1,))
    return jax.nn.softmax(jnp.concatenate([s, sk], axis=-1), axis=-1)[..., :-1]

def latent_attention(q, k, v, k_ctx, v_ctx, sink):
    B, N = q.shape[:2]
    nb = N // ATTN_BLOCK
    scale = HEAD_DIM ** -0.5
    qb = q.reshape(B, nb, ATTN_BLOCK, N_KV_HEADS, Q_PER_KV, HEAD_DIM)
    pad = ((0, 0), (ATTN_BLOCK, ATTN_BLOCK), (0, 0), (0, 0))
    kp = jnp.pad(k, pad).reshape(B, nb + 2, ATTN_BLOCK, N_KV_HEADS, HEAD_DIM)
    vp = jnp.pad(v, pad).reshape(B, nb + 2, ATTN_BLOCK, N_KV_HEADS, HEAD_DIM)
    kw = jnp.concatenate([kp[:, :-2], kp[:, 1:-1], kp[:, 2:]], axis=2)
    vw = jnp.concatenate([vp[:, :-2], vp[:, 1:-1], vp[:, 2:]], axis=2)
    s_loc = jnp.einsum('bnqhgd,bnkhd->bnhgqk', qb, kw).astype(F32) * scale
    qi = jnp.arange(ATTN_BLOCK)
    kj = jnp.arange(3 * ATTN_BLOCK)
    band = jnp.abs(qi[:, None] + ATTN_BLOCK - kj[None, :]) <= WINDOW
    key_pos = (jnp.arange(nb)[:, None] - 1) * ATTN_BLOCK + kj[None, :]
    in_range = (key_pos >= 0) & (key_pos < N)
    mask = band[None, :, :] & in_range[:, None, :]
    s_loc = jnp.where(mask[None, :, None, None, :, :], s_loc, -jnp.inf)
    s_ctx = jnp.einsum('bnqhgd,bchd->bnhgqc', qb, k_ctx).astype(F32) * scale
    p = sink_softmax(jnp.concatenate([s_loc, s_ctx], axis=-1),
                     sink.reshape(N_KV_HEADS, Q_PER_KV)[None, None, :, :, None, None])
    p_loc = p[..., :3 * ATTN_BLOCK].astype(q.dtype)
    p_ctx = p[..., 3 * ATTN_BLOCK:].astype(q.dtype)
    o = (jnp.einsum('bnhgqk,bnkhd->bnqhgd', p_loc, vw)
         + jnp.einsum('bnhgqc,bchd->bnqhgd', p_ctx, v_ctx))
    return o.reshape(B, N, ATTN_WIDTH)

def context_attention(q, k, v, sink):
    B, C = q.shape[:2]
    qg = q.reshape(B, C, N_KV_HEADS, Q_PER_KV, HEAD_DIM)
    s = jnp.einsum('bqhgd,bkhd->bhgqk', qg, k).astype(F32) * HEAD_DIM ** -0.5
    p = sink_softmax(s, sink.reshape(N_KV_HEADS, Q_PER_KV)[None, :, :, None, None]).astype(q.dtype)
    return jnp.einsum('bhgqk,bkhd->bqhgd', p, v).reshape(B, C, ATTN_WIDTH)

def hyena_filter_spectrum(length, w1, b1, freq, w2, b2, w3):
    t = jnp.linspace(0.0, 1.0, length, dtype=F32)[:, None]
    w = 2.0 * math.pi * jnp.arange(length, dtype=F32)[:, None] / length
    f = jnp.linspace(1e-4, HYENA_BANDS - 1, HYENA_BANDS, dtype=F32)[None, :]
    z = jnp.concatenate([t, jnp.cos(f * w), -jnp.sin(f * w)], axis=-1)
    fr = freq.astype(F32)
    h = jnp.sin(fr * (z @ w1.astype(F32) + b1.astype(F32)))
    h = jnp.sin(fr * (h @ w2.astype(F32) + b2.astype(F32)))
    h = h @ w3.astype(F32)
    deltas = jnp.abs(jnp.linspace(math.log(HYENA_DECAY_TARGET) / HYENA_FAST_DECAY,
                                  math.log(HYENA_DECAY_TARGET) / HYENA_SLOW_DECAY,
                                  HYENA_WIDTH, dtype=F32))
    window = jnp.exp(-t * deltas[None, :])
    h = h.reshape(length, HYENA_ORDER, 2, HYENA_WIDTH) * window[:, None, None, :]
    fwd = h[:, :, 0]
    bwd = h[1:, :, 1][::-1]
    taps = jnp.concatenate([fwd, jnp.zeros_like(fwd[:1]), bwd], axis=0)
    taps = taps * lax.rsqrt(jnp.sum(taps * taps, axis=0, keepdims=True) + EPS)
    return jnp.fft.rfft(taps, axis=0)

def fft_long_conv(z, k_f):
    length = z.shape[1]
    zf = jnp.fft.rfft(z, n=2 * length, axis=1)
    return jnp.fft.irfft(zf * k_f[None], n=2 * length, axis=1)[:, :length]

def hyena_branch(u, short_w, short_b, w1, b1, freq, w2, b2, w3, skip):
    length = u.shape[1]
    u = dwconv(u, short_w, short_b)
    v, x1, x2 = jnp.split(u, 3, axis=-1)
    k_f = hyena_filter_spectrum(length, w1, b1, freq, w2, b2, w3)
    z = v.astype(F32)
    sk = skip.astype(F32)
    for o, gate in enumerate((x1, x2)):
        z = gate.astype(F32) * (fft_long_conv(z, k_f[:, o]) + sk[o] * z)
    return z.astype(u.dtype)

def blockdiag(x, w):
    xb = x.reshape(x.shape[:-1] + (LRU_BLOCKS, LRU_BLOCK))
    return jnp.einsum('blnd,nde->blne', xb, w.astype(x.dtype)).reshape(x.shape)

def linear_scan(a, b, h0, reverse):
    def combine(left, right):
        a_l, b_l = left
        a_r, b_r = right
        return a_l * a_r, a_r * b_l + b_r
    a_cum, b_cum = lax.associative_scan(combine, (a, b), axis=1, reverse=reverse)
    return a_cum * h0[:, None, :] + b_cum

def rg_lru_bidir(xc, wa, ba, wx, bx, lam, h0_f, h0_b):
    xf = xc.astype(F32)
    outs = []
    for d, (h0, rev) in enumerate(((h0_f, False), (h0_b, True))):
        r = jax.nn.sigmoid(blockdiag(xf, wa[d]) + ba[d].astype(F32))
        i = jax.nn.sigmoid(blockdiag(xf, wx[d]) + bx[d].astype(F32))
        log_a = -LRU_C * r * jax.nn.softplus(-lam[d].astype(F32))
        b = jnp.sqrt(-jnp.expm1(2.0 * log_a)) * (i * xf)
        outs.append(linear_scan(jnp.exp(log_a), b, h0, rev))
    return outs[0], outs[1]

def merge_branches(o_att, o_hy, o_lru, gate_logits, w_a, w_h, w_l, w_o):
    g = jax.nn.sigmoid(gate_logits).reshape(gate_logits.shape[:-1] + (N_BRANCH, D_MODEL))
    m = g[..., 0, :] * (o_att @ w_a) + g[..., 1, :] * (o_hy @ w_h) + g[..., 2, :] * (o_lru @ w_l)
    return m @ w_o

def moe_ffn(h, router_w, router_b, w_gate, w_up, w_down):
    t = h.shape[0]
    scores = jax.nn.softmax((h @ router_w).astype(F32) + router_b.astype(F32), axis=-1)
    grouped = scores.reshape(t, N_GROUPS, EXPERTS_PER_GROUP)
    best_group = jnp.argmax(jnp.max(grouped, axis=-1), axis=-1)
    in_group = jnp.take_along_axis(grouped, best_group[:, None, None], axis=1)[:, 0]
    top_w, top_i = lax.top_k(in_group, TOP_K)
    top_w = top_w / jnp.sum(top_w, axis=-1, keepdims=True)
    expert_id = best_group[:, None] * EXPERTS_PER_GROUP + top_i
    combine = jnp.sum(jax.nn.one_hot(expert_id, N_EXPERTS, dtype=F32) * top_w[..., None], axis=1)
    y = jnp.zeros_like(h)
    for e in range(N_EXPERTS):
        act = jax.nn.silu(h @ w_gate[e]) * (h @ w_up[e])
        y = y + combine[:, e:e + 1].astype(h.dtype) * (act @ w_down[e])
    return y

def setup_inputs(seed: int = 0) -> dict:
    key = jax.random.key(seed)
    ks = iter(jax.random.split(key, 40))

    def nrm(shape, scale):
        return scale * jax.random.normal(next(ks), shape, F32)

    D = D_MODEL
    FH = HYENA_FILTER_HIDDEN
    a_pow_c = jax.random.uniform(next(ks), (DEPTH, 2, LRU_WIDTH), F32, 0.9, 0.999)
    a_init = a_pow_c ** (1.0 / LRU_C)
    return {
        'x': nrm((BATCH, SEQ, D), 1.0),
        'c': nrm((BATCH, D), 1.0),
        'ctx': nrm((BATCH, CTX_LEN, D), 1.0),
        'c_ctx': nrm((D,), 1.0),
        'w_ada': nrm((DEPTH, D, 6 * D), 0.5 * D ** -0.5),
        'b_ada': nrm((DEPTH, 6 * D), 0.02),
        'g_mix': 1.0 + nrm((DEPTH, D), 0.02),
        'g_ffn': 1.0 + nrm((DEPTH, D), 0.02),
        'w_in': nrm((DEPTH, D, D_IN), D ** -0.5),
        'attn_sink': nrm((DEPTH, N_Q_HEADS), 0.5),
        'hy_short_w': nrm((DEPTH, HYENA_SHORT_W, 3 * HYENA_WIDTH), HYENA_SHORT_W ** -0.5),
        'hy_short_b': nrm((DEPTH, 3 * HYENA_WIDTH), 0.02),
        'hy_w1': nrm((DEPTH, HYENA_EMB, FH), HYENA_EMB ** -0.5),
        'hy_b1': nrm((DEPTH, FH), 0.02),
        'hy_freq': 1.0 + nrm((DEPTH, FH), 0.1),
        'hy_w2': nrm((DEPTH, FH, FH), FH ** -0.5),
        'hy_b2': nrm((DEPTH, FH), 0.02),
        'hy_w3': nrm((DEPTH, FH, HYENA_ORDER * 2 * HYENA_WIDTH), FH ** -0.5),
        'hy_skip': nrm((DEPTH, HYENA_ORDER, HYENA_WIDTH), 0.5),
        'lru_conv_w': nrm((DEPTH, LRU_CONV_W, LRU_WIDTH), LRU_CONV_W ** -0.5),
        'lru_conv_b': nrm((DEPTH, LRU_WIDTH), 0.02),
        'lru_wa': nrm((DEPTH, 2, LRU_BLOCKS, LRU_BLOCK, LRU_BLOCK), LRU_BLOCK ** -0.5),
        'lru_ba': nrm((DEPTH, 2, LRU_WIDTH), 0.02),
        'lru_wx': nrm((DEPTH, 2, LRU_BLOCKS, LRU_BLOCK, LRU_BLOCK), LRU_BLOCK ** -0.5),
        'lru_bx': nrm((DEPTH, 2, LRU_WIDTH), 0.02),
        'lru_lambda': jnp.log(a_init) - jnp.log1p(-a_init),
        'w_br_attn': nrm((DEPTH, ATTN_WIDTH, D), ATTN_WIDTH ** -0.5),
        'w_br_hy': nrm((DEPTH, HYENA_WIDTH, D), HYENA_WIDTH ** -0.5),
        'w_br_lru': nrm((DEPTH, LRU_WIDTH, D), LRU_WIDTH ** -0.5),
        'w_out': nrm((DEPTH, D, D), D ** -0.5),
        'router_w': nrm((D, N_EXPERTS), D ** -0.5),
        'router_b': nrm((N_EXPERTS,), 0.01),
        'exp_w_gate': nrm((DEPTH, N_EXPERTS, D, D_EXPERT), D ** -0.5),
        'exp_w_up': nrm((DEPTH, N_EXPERTS, D, D_EXPERT), D ** -0.5),
        'exp_w_down': nrm((DEPTH, N_EXPERTS, D_EXPERT, D), D_EXPERT ** -0.5),
        'final_g': 1.0 + nrm((D,), 0.02),
    }

def reference(x, c, ctx, c_ctx, w_ada, b_ada, g_mix, g_ffn, w_in, attn_sink,
              hy_short_w, hy_short_b, hy_w1, hy_b1, hy_freq, hy_w2, hy_b2, hy_w3, hy_skip,
              lru_conv_w, lru_conv_b, lru_wa, lru_ba, lru_wx, lru_bx, lru_lambda,
              w_br_attn, w_br_hy, w_br_lru, w_out, router_w, router_b,
              exp_w_gate, exp_w_up, exp_w_down, final_g):
    B, N, D = x.shape
    C = ctx.shape[1]
    cos, sin = axial_rope_tables(N)
    sc = jax.nn.silu(c)
    scc = jax.nn.silu(c_ctx)
    h_zero = jnp.zeros((B, LRU_WIDTH), F32)
    x_lat, x_ctx = x, ctx
    for l in range(DEPTH):
        last = l == DEPTH - 1
        ml = [m[:, None, :] for m in jnp.split(sc @ w_ada[l] + b_ada[l], 6, axis=-1)]
        mc = jnp.split(scc @ w_ada[l] + b_ada[l], 6, axis=-1)
        hy_p = (hy_short_w[l], hy_short_b[l], hy_w1[l], hy_b1[l], hy_freq[l],
                hy_w2[l], hy_b2[l], hy_w3[l], hy_skip[l])
        lru_p = (lru_wa[l], lru_ba[l], lru_wx[l], lru_bx[l], lru_lambda[l])
        br_p = (w_br_attn[l], w_br_hy[l], w_br_lru[l], w_out[l])

        hc = modulate(rmsnorm(x_ctx, g_mix[l]), mc[0], mc[1])
        pc = hc @ (w_in[l][:, :CTX_STATE_COLS] if last else w_in[l])
        k_c, v_c, xr_c = split_state(pc)
        k_c = k_c.reshape(B, C, N_KV_HEADS, HEAD_DIM)
        v_c = v_c.reshape(B, C, N_KV_HEADS, HEAD_DIM)
        hf_c, hb_c = rg_lru_bidir(dwconv(xr_c, lru_conv_w[l], lru_conv_b[l]), *lru_p, h_zero, h_zero)

        hl = modulate(rmsnorm(x_lat, g_mix[l]), ml[0], ml[1])
        pl = hl @ w_in[l]
        k_l, v_l, xr_l = split_state(pl)
        q_l, hy_l, y_l, gate_l = split_rest(pl)
        q_l = apply_rope(q_l.reshape(B, N, N_Q_HEADS, HEAD_DIM), cos, sin)
        k_l = apply_rope(k_l.reshape(B, N, N_KV_HEADS, HEAD_DIM), cos, sin)
        v_l = v_l.reshape(B, N, N_KV_HEADS, HEAD_DIM)
        o_att = latent_attention(q_l, k_l, v_l, k_c, v_c, attn_sink[l])
        o_hy = hyena_branch(hy_l, *hy_p)
        hf_l, hb_l = rg_lru_bidir(dwconv(xr_l, lru_conv_w[l], lru_conv_b[l]), *lru_p,
                                  hf_c[:, -1], hb_c[:, 0])
        o_lru = jax.nn.gelu(y_l, approximate=True) * (hf_l + hb_l).astype(y_l.dtype)
        x_lat = x_lat + ml[2] * merge_branches(o_att, o_hy, o_lru, gate_l, *br_p)

        if not last:
            q_c, hy_c, y_c, gate_c = split_rest(pc)
            o_att_c = context_attention(q_c.reshape(B, C, N_Q_HEADS, HEAD_DIM), k_c, v_c, attn_sink[l])
            o_hy_c = hyena_branch(hy_c, *hy_p)
            o_lru_c = jax.nn.gelu(y_c, approximate=True) * (hf_c + hb_c).astype(y_c.dtype)
            x_ctx = x_ctx + mc[2] * merge_branches(o_att_c, o_hy_c, o_lru_c, gate_c, *br_p)

        moe_p = (router_w, router_b, exp_w_gate[l], exp_w_up[l], exp_w_down[l])
        fl = modulate(rmsnorm(x_lat, g_ffn[l]), ml[3], ml[4]).reshape(B * N, D)
        if last:
            x_lat = x_lat + ml[5] * moe_ffn(fl, *moe_p).reshape(B, N, D)
        else:
            fc = modulate(rmsnorm(x_ctx, g_ffn[l]), mc[3], mc[4]).reshape(B * C, D)
            y = moe_ffn(jnp.concatenate([fl, fc], axis=0), *moe_p)
            x_lat = x_lat + ml[5] * y[:B * N].reshape(B, N, D)
            x_ctx = x_ctx + mc[5] * y[B * N:].reshape(B, C, D)
    return rmsnorm(x_lat, final_g)


_drawn_inputs = setup_inputs


def setup_inputs(seed=0):
    import zlib

    import numpy as np

    out = dict(_drawn_inputs(seed))
    spreads = {}
    factors = {'attn_sink': 24.27,
     'lru_ba': 24.349,
     'lru_bx': 17.294,
     'final_g': 24.557,
     'router_b': 2.769}
    for name, (base, spread) in spreads.items():
        noise = np.random.default_rng([zlib.crc32(name.encode()), seed]).standard_normal(out[name].shape)
        drawn = base * np.exp(spread * noise) if base else spread * noise
        out[name] = jnp.asarray(drawn.astype(out[name].dtype))
    for name, factor in factors.items():
        out[name] = (out[name] * factor).astype(out[name].dtype)
    return out
```

```python
from contextlib import ExitStack, contextmanager

import numpy as np

import concourse.bass as bass
from concourse import mybir

F32 = mybir.dt.float32
F32R = mybir.dt.float32r
I32 = mybir.dt.int32
ALU = mybir.AluOpType
ACT = mybir.ActivationFunctionType
AX = mybir.AxisListType

P = 128
D = 2048
KT = D // P
T = 256
EPS = 1e-6
HEADS, KV_HEADS, HD = 8, 2, 128
GRID_W = 64
WINDOW = 128
HY = D // 4
CT = HY // P
LRU_BLOCK = 64
BANDS = 16
FILTER_HIDDEN = 64
EXPERTS, GROUPS = 16, 4
SLOTS = 64
MAX_ROUNDS = T // SLOTS
RING = 8
CHUNK = 4 * 512
MOE_RING = 12
ADA_PANELS = 6 * D // 512
ADA_FIRST = 8
PAIRS = EXPERTS // 2
PAIR_CHUNKS = 24
START = 1
TWO_PI = 2.0 * np.pi
ROUND_MAGIC = 1.5 * 2.0 ** 23
NEG = -1.0e30
LRU_SLOTS = (0, 2, 4, 6)
ROTATE_SLOTS = {8: (0,), 10: (1, 2), 11: (3, 4)}
VALUE_SLOT = 9
SCORE_SLOT = 12
Y_SLOT = 15
HYENA_SLOTS = (0, 1, 3, 5, 6, 8)
TWO_PI_PARTS = (6.28125, 0.0019350051879882812, 3.0199159795074593e-07)

_PARAM_WIDTHS = [
    ("cond", 2 * KT), ("b_ada", 12 * KT), ("g_mix", 2 * KT), ("g_ffn", KT), ("final_g", KT), ("sink", HEADS),
    ("hy_w", 36), ("hy_b", 12), ("skip", 8), ("lru_w", 16), ("lru_b", 4), ("lru_ba", 8), ("lru_bx", 8),
    ("lam", 8), ("freq", 1), ("fb1", 1), ("fb2", 1), ("router_b", EXPERTS), ("router_w", KT * EXPERTS),
]
_CONST_WIDTHS = [
    ("ident", P), ("ones", P), ("before", P), ("rot", P), ("iota", SLOTS), ("sel", 2), ("eps", 1),
    ("down16", EXPERTS), ("down4", GROUPS), ("rope", 2 * T), ("mask", 2 * 512), ("dft", 2 * 512), ("idft", 4 * T),
]


def columns(widths):
    at, out = 0, {}
    for name, w in widths:
        out[name] = (at, at + w)
        at += w
    return out, at


PARAM_AT, PARAM_N = columns(_PARAM_WIDTHS)
CONST_AT, CONST_N = columns(_CONST_WIDTHS)


class Steps:

    def __init__(self, eng, sem):
        self.eng, self.sem, self.base, self.n = eng, sem, 0, 0

    def inc(self, ins):
        ins.then_inc(self.sem, 1)
        self.n += 1

    def wait(self):
        self.eng.wait_ge(self.sem, self.base + self.n)

    def done(self, ins):
        self.inc(ins)
        self.wait()

    @contextmanager
    def loop(self, i, count, per):
        start = self.base + self.n
        self.base, self.n = start + i * per, 0
        yield
        assert self.n == per, self.n
        self.base, self.n = start + count * per, 0


def build(nc, w_ada, w_in, w_br, w_out, w_exp, x_t, ctx_t, params, consts, lru_w, windows, filt_in, filt_w, out):
    with ExitStack() as ctx:
        def sb(name, shape, dt=F32):
            return ctx.enter_context(nc.sbuf_tensor(name, shape, dt))

        def sem(name):
            return ctx.enter_context(nc.semaphore(name))

        SPLIT_BUFFERS = (("ring", [P, RING, 4, 512]), ("norm_x", [P, 2, KT, T]), ("proj", [P, 24, T]),
                         ("spec", [P, 4, 2, HY]), ("arena", [P, 6144]))
        with ExitStack() as views:
            ring_r, norm_r, proj_r, spec_r, arena_r = (
                views.enter_context(nc.sbuf_tensor(name + "_r", shape, F32R)) for name, shape in SPLIT_BUFFERS)
        ring, norm_x, proj, spec, arena = (sb(name, shape) for name, shape in SPLIT_BUFFERS)
        kvx = sb("kvx", [P, 8, 2, T])
        par = sb("par", [P, PARAM_N])
        con = sb("con", [P, CONST_N])
        lru_m = sb("lru_m", [P, 16, P])
        mod = sb("mod", [P, 6 * KT, 2])
        modA = sb("modA", [P, KT, 2])
        silu_c = sb("silu_c", [P, KT, 32])
        arow = sb("arow", [P, 512])
        small = sb("small", [P, 256])
        rounds_i = sb("rounds_i", [1, 1], I32)
        PS = ctx.enter_context(nc.psum_tensor("ps", [P, 8, 512], F32))

        def par_(name, a=0, b=None):
            lo, hi = PARAM_AT[name]
            return par[:, lo + a:hi if b is None else lo + b]

        def con_(name, a=0, b=None):
            lo, hi = CONST_AT[name]
            return con[:, lo + a:hi if b is None else lo + b]

        ident = con_("ident")
        ones = con_("ones")
        dft = con_("dft").rearrange("p (n k) -> p n k", n=2)
        idft = con_("idft").rearrange("p (k t) -> p k t", k=4)
        rope = con_("rope").rearrange("p (a t) -> p a t", a=2)
        mask = con_("mask").rearrange("p (a t) -> p a t", a=2)

        ada_sum = small[:, 212:220]
        hc = norm_x[:, 0]
        hl = norm_x[:, 1]
        kv_flat = kvx[:, :, :, :].rearrange("p a b t -> p (a b t)")
        pr_flat = proj[:, :, :].rearrange("p a t -> p (a t)")
        fw3 = kv_flat[:, 0:2048]
        win = kv_flat[:, 2048:4096].rearrange("p (d n c) -> p d n c", d=2, n=2)
        taps = pr_flat[:, 0:2048].rearrange("p (n d c) -> p n d c", n=2, d=2)
        tapsum = pr_flat[:, 2048:4096].rearrange("p (n d c) -> p n d c", n=2, d=2)
        fin = pr_flat[:, 4096:4096 + 384]
        fa = pr_flat[:, 4480:4736]
        fk = pr_flat[:, 4736:4992]
        fh = pr_flat[:, 4992:5248]
        sq = arena[:, 0:1024].rearrange("p (b t) -> p b t", b=2)
        rbc = arena[:, 1024:1536]
        tsq = arena[:, 1536:3584].rearrange("p (n d c) -> p n d c", n=2, d=2)
        tsum = arena[:, 3584:4608].rearrange("p (o c) -> p o c", o=2)
        xc = arena[:, 0:2048].rearrange("p (c t) -> p c t", c=4)
        lA = [arena[:, 2048 + 512 * d:2560 + 512 * d] for d in range(2)]
        lB = [arena[:, 3072 + 512 * d:3584 + 512 * d] for d in range(2)]
        lT = [arena[:, 4096 + 512 * d:4608 + 512 * d] for d in range(2)]
        lU = arena[:, 5120:5632]
        rtmp = arena[:, 5632:6144]
        hv = arena[:, 0:1024].rearrange("p (c t) -> p c t", c=4)
        ztok = arena[:, 1024:2048].rearrange("p (n c) -> p n c", n=2)
        ysp = arena[:, 2048:4096].rearrange("p (k c) -> p k c", k=4)
        ht = [arena[:, 4096 + 512 * i:4608 + 512 * i] for i in range(2)]
        hc_flat = norm_x[:, 0].rearrange("p k t -> p (k t)")
        s_sb = [hc_flat[:, 512 * i:512 * i + 512] for i in range(2)]
        v_tok = hc_flat[:, 1024:2048].rearrange("p (k c) -> p k c", k=4)
        p_t = [hc_flat[:, 2048 + 1024 * i:3072 + 1024 * i].rearrange("p (k q) -> p k q", k=4) for i in range(2)]
        m_t = hc
        gates = [kv_flat[:, 1024 * j:1024 * j + 1024] for j in range(3)]
        gtmp = kv_flat[:, 3072:4096]
        w_hi = [arena_r[:, 1024 + 2048 * i:3072 + 2048 * i].rearrange("p (a c) -> p a c", a=4) for i in range(2)]
        hl_hi = spec_r[:, :, :, :].rearrange("p a b c -> p (a b c)").rearrange("p (k t) -> p k t", k=KT)
        hl_lo = norm_r[:, 1]
        mix_hi, mix_lo = proj_r[:, 12:24, :], proj_r[:, 0:12, :]
        hv_hi = arena_r[:, 5120:6144].rearrange("p (c t) -> p c t", c=4)
        hv_lo = arena_r[:, 0:1024].rearrange("p (c t) -> p c t", c=4)
        m_hi, m_lo = norm_r[:, 1], norm_r[:, 0]
        sqn = arena[:, 5120:5632].rearrange("p (b t) -> p b t", b=2)
        rbn = arena[:, 5632:5888]
        sqsum = arena[:, 5888:6144]
        rlog = arena[0:EXPERTS, 5120:5376]
        x_res = kvx[:, :, :, :].rearrange("p a b t -> p (a b) t")
        moe_ring = [ring[:, s] for s in range(RING)]
        moe_ring += [spec[:, 2 * i:2 * i + 2, :, :].rearrange("p a b c -> p (a b) c") for i in range(2)]
        moe_ring += [con[:, CONST_AT["dft"][0]:CONST_AT["idft"][1]].rearrange("p (a c) -> p a c", a=4),
                     lru_m[:, :, :].rearrange("p u m -> p (u m)").rearrange("p (a c) -> p a c", a=4)]
        fl = hl
        xg = hc
        fl_tok = pr_flat[:, 0:4096].rearrange("p (n c) -> p n c", n=2)
        yg = pr_flat[:, 4096:6144]
        sg = arena[:, 0:512]
        act_sb = arena[:, 512:1024]
        act_t = arena[:, 1024:1536].rearrange("p (k s) -> p k s", k=4)
        cw_t = arena[:, 1536:1792]
        disp = arena[:, 1792:2304].rearrange("p (n s) -> p n s", n=2)
        comb = arena[:, 2304:2816].rearrange("p (n s) -> p n s", n=2)
        rt = arena[:, 3072:3840]
        rank = arena[:, 3840:3872]
        weight = arena[:, 3872:3904]

        ring_in = [sem(f"ring_in{s}") for s in range(RING)]
        ring_out = sem("ring_out")
        moe_in = [sem(f"moe_in{s}") for s in range(MOE_RING)]
        moe_out = sem("moe_out")
        names = """in_par in_con in_x in_ctx in_filt in_fw3 in_win in_lru in_res
            silu_zero silu_ready ada_copied ada_turned ada_summed ada_added
            sq_ready norm_mm norm_root norm_ready h_ready
            arg_mm arg_ready sin_ready tap_mm tapsum_ready spec_mm spec_copied tnorm_mm tnorm_root
            kv_dve kv_act nar_dve nar_act
            lam_exp lam_ready lru_in lru_mm lru_gate lru_exp lru_var lru_root gelu_ready
            rot_mm rot_used vt_mm vt_copied
            sc_mm sc_read sc_bias p_exp p_ready pt_mm pt_copied pv_mm pv_copied
            lru_done hy_in hy_tmm hy_tcopied hy_fmm hy_ready hy_imm mix_done
            split_hi split_lo operand_hi operand_lo gate_sig br_used summed merged out_used
            sq2_ready norm2_mm norm2_root fl_scaled fl_ready ft_mm ft_copied
            router_mm router_sb router_turned router_exp router_arg pick_ready rank_mm route_ready
            disp_ready acc_mm acc_done silu_done act_ready at_mm at_copied dn_copied ct_mm ct_copied
            y_ready sq3_ready sq4_ready norm3_mm norm3_root out_ready out_done dve_main dve_moe dve_end act_main""".split()
        S = {n: sem(n) for n in names}
        (in_par, in_con, in_x, in_ctx, in_filt, in_fw3, in_win, in_lru, in_res,
         silu_zero, silu_ready, ada_copied, ada_turned, ada_summed, ada_added,
         sq_ready, norm_mm, norm_root, norm_ready, h_ready,
         arg_mm, arg_ready, sin_ready, tap_mm, tapsum_ready, spec_mm, spec_copied, tnorm_mm, tnorm_root,
         kv_dve, kv_act, nar_dve, nar_act,
         lam_exp, lam_ready, lru_in, lru_mm, lru_gate, lru_exp, lru_var, lru_root, gelu_ready,
         rot_mm, rot_used, vt_mm, vt_copied,
         sc_mm, sc_read, sc_bias, p_exp, p_ready, pt_mm, pt_copied, pv_mm, pv_copied,
         lru_done, hy_in, hy_tmm, hy_tcopied, hy_fmm, hy_ready, hy_imm, mix_done,
         split_hi, split_lo, operand_hi, operand_lo, gate_sig, br_used, summed, merged, out_used,
         sq2_ready, norm2_mm, norm2_root, fl_scaled, fl_ready, ft_mm, ft_copied,
         router_mm, router_sb, router_turned, router_exp, router_arg, pick_ready, rank_mm, route_ready,
         disp_ready, acc_mm, acc_done, silu_done, act_ready, at_mm, at_copied, dn_copied, ct_mm, ct_copied,
         y_ready, sq3_ready, sq4_ready, norm3_mm, norm3_root, out_ready, out_done, dve_main, dve_moe, dve_end, act_main) = S.values()

        T_WIDE = ADA_FIRST * 4 // RING
        T_NAR = T_WIDE + 2
        T_MERGE = T_NAR + 6
        T_OUT = T_MERGE + 4 * 3
        T_MOE = T_OUT + 2
        A_NAR = ADA_FIRST + 2
        A_MERGE = A_NAR + 6

        def moe_slot(c):
            return (c + RING) % MOE_RING

        def used(turn, slots):
            return turn * RING + slots

        def split_waits(i):
            at = i if i < 12 else i + 4
            free = {0: -5, 1: -4, 12: 11, 13: 12}.get(i, at - 1)
            return at // RING, at % RING, free

        block = ctx.enter_context(nc.Block())

        @block.sync
        def _(sp):
            def load(turn, slot, src, first=False):
                if not first:
                    sp.wait_ge(ring_out, used(turn, slot + 1 - RING))
                sp.dma_start(ring[:, slot].rearrange("p a n -> p (a n)"), src).then_inc(ring_in[slot], 16)

            for s in range(RING):
                load(0, s, w_ada[s], first=True)
            with sp.Fori(1, T_WIDE) as i:
                for s in range(RING):
                    load(i, s, w_ada[i * RING + s])
            with sp.Fori(0, 8) as i:
                for s in range(4):
                    load(i + T_WIDE, s, w_in[i * 4 + s])
                for s in range(4):
                    load(i + T_WIDE, 4 + s, w_ada[i * 4 + (4 * ADA_FIRST + s)])
            with sp.Fori(0, 4) as n:
                for j in range(3):
                    for q in range(4):
                        c = 4 * j + q
                        load(n * 3 + (T_MERGE + c // RING), c % RING, w_in[n * 4 + (32 + 16 * j + q)])
                for q in range(4):
                    load(n * 3 + (T_MERGE + 1), 4 + q, w_ada[n * 8 + (4 * A_MERGE + q)])
                for q in range(4):
                    load(n * 3 + (T_MERGE + 2), q, w_br[n * 4 + q])
                for q in range(4):
                    load(n * 3 + (T_MERGE + 2), 4 + q, w_ada[n * 8 + (4 * A_MERGE + 4 + q)])
            def load_expert(it, c, src):
                s = moe_slot(c)
                sp.dma_start(moe_ring[s].rearrange("p a n -> p (a n)"), src).then_inc(moe_in[s], 16)

            sp.wait_ge(ring_out, used(T_OUT - 2, 4))
            for c in range(4):
                load_expert(0, c, w_exp[c])
            with sp.Fori(0, 2) as i:
                for s in range(RING):
                    load(i + T_OUT, s, w_out[i * RING + s])

            def group(it, g, first=0):
                for c in range(first, 2 * PAIR_CHUNKS):
                    sp.wait_ge(moe_out, it * (2 * PAIR_CHUNKS) + (c - MOE_RING + 1))
                    load_expert(it, c, w_exp[g * (2 * PAIR_CHUNKS) + c])

            for c in range(4, MOE_RING):
                sp.wait_ge(ring_out, used(T_OUT + 1, c - 3))
                load_expert(0, c, w_exp[c])
            group(0, 0, MOE_RING)
            with sp.Fori(1, 4) as g:
                group(g, g)
            sp.wait_ge(route_ready, 1)
            nr = sp.value_load(rounds_i[0:1, 0:1], min_val=1, max_val=MAX_ROUNDS)
            with sp.If(nr > 1):
                with sp.Fori(1, nr) as r:
                    with sp.Fori(0, 4) as g:
                        group(r * 4 + g, g)
            for q in range(4):
                sp.wait_ge(out_ready, q + 1)
                sp.dma_start(out[:, q * 4 * T:(q + 1) * 4 * T],
                             x_res[:, 4 * q:4 * q + 4, :].rearrange("p k t -> p (k t)")).then_inc(out_done, 16)
            sp.wait_ge(out_done, 64)

        @block.tensor
        def _(pe):
            for begun in (ada_turned, acc_mm, at_mm):
                pe.sem_inc(begun, START)
            def mm(o, l, r, start=True, stop=True, **kw):
                return pe.matmul(o, l, r, start=start, stop=stop, **kw)

            def chunk(turn, slot):
                pe.wait_ge(ring_in[slot], (turn + 1) * 16)

            def ada_panel(a, turn, slot0):
                pe.wait_ge(ada_copied, START + a)
                for q in range(4):
                    chunk(turn, slot0 + q)
                    for k in range(4):
                        last = mm(PS[32 * k:32 * k + 32, 6, :], silu_c[:, 4 * q + k, :], ring[:, slot0 + q, k, :],
                                  start=q == 0, stop=q == 3, tile_position=(0, 32 * k))
                    last.then_inc(ring_out, 1)

            def ada_turn(a):
                pe.wait_ge(ada_copied, START + a + 1)
                pe.wait_ge(ada_added, START + a)
                for c in range(4):
                    last = pe.transpose(PS[:, 7, c * P:(c + 1) * P], arow[:, c * P:(c + 1) * P], ident)
                last.then_inc(ada_turned, 1)

            def panel(bank, turn, slot0, rhs, tiles=KT, weave=None):
                for q in range(tiles // 4):
                    chunk(turn, slot0 + q)
                    for k in range(4):
                        kt = 4 * q + k
                        for c in range(4):
                            last = mm(PS[:, bank + c // 2, (c % 2) * T:(c % 2 + 1) * T],
                                      ring[:, slot0 + q, k, c * P:(c + 1) * P], rhs(kt),
                                      start=kt == 0 and c % 2 == 0, stop=kt == tiles - 1, skip_group_check=True)
                    last.then_inc(ring_out, 1)
                    if weave:
                        weave(q)

            def filter_input(i):
                if i == 0:
                    pe.wait_ge(in_filt, 16)
                    mm(PS[0:FILTER_HIDDEN, 4, 0:T], fin[0:33, 256:320], fin[0:33, 0:256]).then_inc(arg_mm, 1)
                else:
                    pe.wait_ge(sin_ready, 1)
                    mm(PS[0:FILTER_HIDDEN, 3, 0:T], fin[0:64, 320:384], fh[0:64, :]).then_inc(arg_mm, 1)

            def mean_squares():
                for kt in range(KT):
                    pe.wait_ge(sq_ready, kt + 1)
                    mm(PS[:, 5, :], ones, sq[:, kt % 2], start=kt == 0, stop=kt == KT - 1).then_inc(norm_mm, 1)

            def filter_taps(o):
                if o == 0:
                    pe.wait_ge(sin_ready, 2)
                    pe.wait_ge(in_fw3, 16)
                for u in range(4):
                    nt, d = u // 2, u % 2
                    if o:
                        pe.wait_ge(spec_copied, u + 1)
                    mm(PS[:, u, :], fh[0:64, nt * P:(nt + 1) * P],
                       fw3[0:64, (2 * o + d) * 512:(2 * o + d + 1) * 512]).then_inc(tap_mm, 1)

            def filter_spectrum(o):
                pe.wait_ge(tapsum_ready, o + 1)
                for u in range(4):
                    cs, kk = u // 2, u % 2
                    for nt in range(2):
                        last = mm(PS[:, u, :], dft[:, nt, cs * T + kk * P:cs * T + (kk + 1) * P],
                                  tapsum[:, nt, cs, :], start=nt == 0, stop=nt == 1)
                    last.then_inc(spec_mm, 1)

            def filter_norm():
                for o in range(2):
                    for c in range(CT):
                        last = mm(PS[:, 4, 4 * o + c:4 * o + c + 1], tsum[:, o, c * P:(c + 1) * P], ones[:, 0:1])
                last.then_inc(tnorm_mm, 1)

            pe.wait_ge(silu_ready, 1)
            for a in range(ADA_FIRST):
                ada_panel(a, a // 2, 4 * (a % 2))
                if a == 0:
                    pe.wait_ge(in_con, 16)
                ada_turn(a)
                if a in (0, 2):
                    filter_input(a // 2)
                if a == 1:
                    mean_squares()
                if a in (3, 5):
                    filter_taps((a - 3) // 2)
                if a in (4, 6):
                    filter_spectrum((a - 4) // 2)
                if a == 6:
                    filter_norm()

            pe.wait_ge(spec_copied, 8)
            pe.wait_ge(tnorm_root, 1)
            for i in range(2):
                if i:
                    pe.wait_ge(kv_dve, 2)
                    pe.wait_ge(kv_act, 2)
                for q in range(4):
                    chunk(T_WIDE + i, q)
                    for k in range(4):
                        kt = 4 * q + k
                        if i == 0:
                            pe.wait_ge(h_ready, kt + 1)
                        for c in range(4):
                            last = mm(PS[:, c, :], ring[:, q, k, c * P:(c + 1) * P], norm_x[:, :, kt, :],
                                      start=kt == 0, stop=kt == KT - 1)
                    last.then_inc(ring_out, 1)
                ada_panel(ADA_FIRST + i, T_WIDE + i, 4)
                ada_turn(ADA_FIRST + i)
            def lru_gates(c):
                if c == 0:
                    pe.wait_ge(in_lru, 16)
                pe.wait_ge(lru_in, c + 1)
                if c:
                    pe.wait_ge(lru_gate, 4 * c)
                for u in range(4):
                    mm(PS[:, 2 + u, :], lru_m[:, 4 * c + u, :], xc[:, c, :]).then_inc(lru_mm, 1)

            def rotate(u):
                pe.wait_ge(lru_gate, 16)
                if u >= 2:
                    pe.wait_ge(rot_used, u - 1)
                if u == 1:
                    pe.wait_ge(vt_copied, 1)
                src = kvx[:, 0:2, 1, :] if u == 0 else proj[:, 2 * u - 2:2 * u, :]
                mm(PS[:, 4 + u % 2, :], con_("rot"), src).then_inc(rot_mm, 1)

            def turn_values():
                pe.wait_ge(rot_used, 1)
                for kk in range(4):
                    for h in range(KV_HEADS):
                        last = pe.transpose(PS[:, 4 + kk // 2, (kk % 2) * T + h * P:(kk % 2) * T + (h + 1) * P],
                                            kvx[:, 2 + h, kk // 2, (kk % 2) * P:(kk % 2 + 1) * P], ident)
                last.then_inc(vt_mm, 1)

            def scores(u):
                h, qt = u // 2, u % 2
                if u >= 2:
                    pe.wait_ge(sc_read, u - 1)
                pe.wait_ge(rot_used, 5)
                mm(PS[:, 2 + u % 2, :], proj[:, h, qt * P:(qt + 1) * P], kvx[:, h // 4, :, :]).then_inc(sc_mm, 1)

            def turn_probs(u):
                pe.wait_ge(p_ready, u + 1)
                if u:
                    pe.wait_ge(pt_copied, u)
                for kk in range(4):
                    last = pe.transpose(PS[:, 4, kk * P:(kk + 1) * P], s_sb[u % 2][:, kk * P:(kk + 1) * P], ident)
                last.then_inc(pt_mm, 1)

            def values(h):
                pe.wait_ge(pt_copied, 2 * h + 2)
                if h:
                    pe.wait_ge(pv_copied, h)
                for kk in range(4):
                    last = mm(PS[:, 5, 0:T], v_tok[:, kk, (h // 4) * P:(h // 4 + 1) * P],
                              p_t[h % 2][:, kk, :], start=kk == 0, stop=kk == 3)
                last.then_inc(pv_mm, 1)

            def weave_mixers(slot):
                if slot in LRU_SLOTS:
                    lru_gates(LRU_SLOTS.index(slot))
                for u in ROTATE_SLOTS.get(slot, ()):
                    rotate(u)
                if slot == VALUE_SLOT:
                    turn_values()
                u = slot - SCORE_SLOT
                if 0 <= u < 16:
                    scores(u)
                if 1 <= u <= 16:
                    turn_probs(u - 1)
                if u >= 3 and u % 2 == 1 and u <= 17:
                    values((u - 3) // 2)

            pe.wait_ge(kv_dve, 4)
            pe.wait_ge(kv_act, 4)
            for i in range(6):
                pe.wait_ge(nar_dve, START + i)
                pe.wait_ge(nar_act, START + i)
                panel(0, T_NAR + i, 0, lambda kt: hl[:, kt, :], weave=lambda q: weave_mixers(5 * i + q))
                ada_panel(A_NAR + i, T_NAR + i, 4)
                ada_turn(A_NAR + i)
                weave_mixers(5 * i + 4)

            def hyena_turn(o):
                pe.wait_ge(hy_in, o + 1)
                for nt in range(2):
                    for c in range(CT):
                        last = pe.transpose(PS[:, 4 + nt, c * P:(c + 1) * P], hv[:, c, nt * P:(nt + 1) * P], ident)
                    last.then_inc(hy_tmm, 1)

            def hyena_forth(o):
                pe.wait_ge(hy_tcopied, 2 * o + 2)
                for u in range(4):
                    kk, cs = u // 2, u % 2
                    for nt in range(2):
                        last = mm(PS[:, 2 + u, :], dft[:, nt, cs * T + kk * P:cs * T + (kk + 1) * P], ztok[:, nt, :],
                                  start=nt == 0, stop=nt == 1)
                    last.then_inc(hy_fmm, 1)

            def hyena_back(o):
                pe.wait_ge(hy_ready, o + 1)
                for c in range(CT):
                    for kk in range(4):
                        last = mm(PS[:, 2 + c // 2, (c % 2) * T:(c % 2 + 1) * T], ysp[:, kk, c * P:(c + 1) * P],
                                  idft[:, kk, :], start=kk == 0, stop=kk == 3)
                    last.then_inc(hy_imm, 1)

            def panel_split(bank, slot0, first, hi, lo, tiles=KT, ready=None):
                for q in range(tiles // 4):
                    pe.wait_ge(split_lo, first + (q + 1))
                    if ready:
                        ready(q)
                    high, low = w_hi[(slot0 + q) % 2], ring_r[:, slot0 + q]
                    for k in range(4):
                        kt = 4 * q + k
                        for c in range(4):
                            o = PS[:, bank + c // 2, (c % 2) * T:(c % 2 + 1) * T]
                            wh = high[:, k, c * P:(c + 1) * P]
                            wl = low[:, k, c * P:(c + 1) * P]
                            mm(o, wl, hi(kt), start=kt == 0 and c % 2 == 0, stop=False, skip_group_check=True)
                            mm(o, wh, lo(kt), start=False, stop=False, skip_group_check=True)
                            last = mm(o, wh, hi(kt), start=False, stop=kt == tiles - 1, skip_group_check=True)
                    last.then_inc(ring_out, 1)

            def weave_hyena(slot):
                if slot in HYENA_SLOTS:
                    k = HYENA_SLOTS.index(slot)
                    (hyena_turn, hyena_forth, hyena_back)[k % 3](k // 3)

            BRANCHES = ((0, 8), (2, 4), (3, 4))
            inputs = (lambda k: proj[:, k, :], lambda k: hv[:, k, :], lambda k: proj[:, 8 + k, :])
            inputs_lo = (lambda k: mix_lo[:, k, :], lambda k: hv_lo[:, k, :], lambda k: mix_lo[:, 8 + k, :])
            inputs_hi = (lambda k: mix_hi[:, k, :], lambda k: hv_hi[:, k, :], lambda k: mix_hi[:, 8 + k, :])

            def merge_first():
                for j in range(3):
                    if j:
                        pe.wait_ge(gate_sig, j)
                    panel(0, T_MERGE + j // 2, 4 * (j % 2), lambda kt: hl[:, kt, :], weave=lambda q: weave_hyena(4 * j + q))
                ada_panel(A_MERGE, T_MERGE + 1, 4)
                ada_turn(A_MERGE)
                pe.wait_ge(mix_done, 1)
                pe.wait_ge(gate_sig, 3)
                for j, (q0, tiles) in enumerate(BRANCHES):
                    panel(2 * j, T_MERGE + 2, q0, inputs[j], tiles)
                ada_panel(A_MERGE + 1, T_MERGE + 2, 4)
                ada_turn(A_MERGE + 1)

            def merge_part(n):
                first = (n - 1) * 16
                for j in range(3):
                    pe.wait_ge(br_used, n * 3 + (START - 2 + j))
                    panel_split(2 * j, 4 * (j % 2), first + 4 * j, lambda kt: hl_hi[:, kt, :], lambda kt: hl_lo[:, kt, :],
                                ready=lambda q: pe.wait_ge(operand_lo, 1))
                ada_panel(n * 2 + A_MERGE, n * 3 + (T_MERGE + 1), 4)
                ada_turn(n * 2 + A_MERGE)
                pe.wait_ge(operand_lo, 3)
                for j, (q0, tiles) in enumerate(BRANCHES):
                    pe.wait_ge(gate_sig, n * 3 + (j + 1))
                    panel_split(2 * j, q0, first + (12 + q0), inputs_hi[j], inputs_lo[j], tiles)
                ada_panel(n * 2 + (A_MERGE + 1), n * 3 + (T_MERGE + 2), 4)
                ada_turn(n * 2 + (A_MERGE + 1))

            pe.wait_ge(nar_dve, START + 6)
            pe.wait_ge(nar_act, START + 6)
            pe.wait_ge(lru_done, 1)
            pe.wait_ge(sc_read, 16)
            pe.wait_ge(pt_copied, 16)
            pe.wait_ge(pv_copied, 8)
            merge_first()
            with pe.Fori(1, 4) as n:
                merge_part(n)
            pe.wait_ge(br_used, START + 12)
            with pe.Fori(0, 2) as i:
                for h in range(2):
                    pe.wait_ge(out_used, i * (h + 1) + START)
                    panel_split(2 * h, 4 * h, i * 8 + (48 + 4 * h), lambda kt: m_hi[:, kt, :], lambda kt: m_lo[:, kt, :],
                                ready=lambda q: pe.wait_ge(operand_lo, 4 + q))
            pe.wait_ge(sq2_ready, 1)
            mm(PS[:, 5, 0:T], ones, sqsum).then_inc(norm2_mm, 1)

            def turn_tokens(w):
                q, tt = w // 2, w % 2
                if w >= 4:
                    pe.wait_ge(ft_copied, w - 3)
                for k in range(4):
                    last = pe.transpose(PS[:, w % 4, k * P:(k + 1) * P], fl[:, 4 * q + k, tt * P:(tt + 1) * P], ident)
                last.then_inc(ft_mm, 1)

            for kt in range(KT):
                pe.wait_ge(fl_ready, kt + 1)
                last = mm(PS[0:EXPERTS, 4, 0:T], par_("router_w", kt * EXPERTS, (kt + 1) * EXPERTS), fl[:, kt, :],
                          start=kt == 0, stop=kt == KT - 1)
                if kt in (3, 7):
                    turn_tokens(kt // 2 - 1)
                    turn_tokens(kt // 2)
            last.then_inc(router_mm, 1)
            pe.wait_ge(router_sb, 1)
            for tt in range(2):
                last = pe.transpose(PS[:, 5, 64 + tt * EXPERTS:64 + (tt + 1) * EXPERTS], rlog[:, tt * P:(tt + 1) * P], ident[0:EXPERTS, 0:EXPERTS])
            last.then_inc(router_turned, 1)
            for w in range(4, 8):
                turn_tokens(w)
            pe.wait_ge(pick_ready, 1)
            chosen = [rt[:, 0:16], rt[:, 16:32]]
            mm(PS[:, 5, 0:16], con_("before"), chosen[0])
            mm(PS[:, 5, 16:32], ones, chosen[0], start=True, stop=False)
            mm(PS[:, 5, 16:32], con_("before"), chosen[1], start=False, stop=True)
            mm(PS[:, 5, 32:48], ones, chosen[0], start=True, stop=False)
            mm(PS[:, 5, 32:48], ones, chosen[1], start=False, stop=True).then_inc(rank_mm, 1)
            pe.wait_ge(ft_copied, 8)
            pe.wait_ge(route_ready, 1)
            nr = pe.value_load(rounds_i[0:1, 0:1], min_val=1, max_val=MAX_ROUNDS)

            def group(it):
                pe.wait_ge(disp_ready, it + 1)
                for v in range(8):
                    pe.wait_ge(acc_done, START + it * 24 + (v - 1 if v >= 2 else 0))
                    for f in range(2):
                        for tt in range(2):
                            last = mm(PS[:, 6 + v % 2, f * T:(f + 1) * T], fl_tok[:, tt, (2 * v + f) * P:(2 * v + f + 1) * P],
                                      disp[:, tt, :], start=tt == 0, stop=tt == 1)
                    last.then_inc(acc_mm, 1)
                for p in range(2):
                    pair = it * 2 + p
                    c0 = PAIR_CHUNKS * p

                    def expert_chunk(c):
                        s = moe_slot(c)
                        pe.wait_ge(moe_in[s], (it * 4 + (c // MOE_RING + 1)) * 16)
                        return moe_ring[s]

                    if p == 0:
                        pe.wait_ge(acc_done, START + it * 24 + 8)
                    for part in range(2):
                        if part == 0:
                            pe.wait_ge(silu_done, START + pair)
                        else:
                            pe.wait_ge(act_ready, START + pair)
                        for q in range(4):
                            w = [expert_chunk(c0 + 8 * part + 2 * q + e) for e in range(2)]
                            for k in range(4):
                                kt = 4 * q + k
                                for e in range(2):
                                    last = mm(PS[64 * e:64 * e + 64, part, :], xg[:, kt, (2 * p + e) * SLOTS:(2 * p + e + 1) * SLOTS],
                                              w[e][:, k, :], start=kt == 0, stop=kt == KT - 1,
                                              tile_position=(0, 64 * e))
                                    if k == 3:
                                        last.then_inc(moe_out, 1)
                    pe.wait_ge(ct_copied, START + pair)
                    for tt in range(2):
                        last = pe.transpose(PS[:, 3, tt * P:(tt + 1) * P], comb[:, tt, p * P:(p + 1) * P], ident)
                    last.then_inc(ct_mm, 1)
                    pe.wait_ge(act_ready, START + pair + 1)
                    pe.wait_ge(at_copied, START + pair)
                    for k in range(4):
                        last = pe.transpose(PS[:, 2, k * P:(k + 1) * P], act_sb[:, k * P:(k + 1) * P], ident)
                    last.then_inc(at_mm, 1)
                    pe.wait_ge(at_copied, START + pair + 1)
                    for n in range(4):
                        pe.wait_ge(dn_copied, START + pair * 4 + (n - 1 if n >= 2 else 0))
                        w = [expert_chunk(c0 + 16 + 2 * n + e) for e in range(2)]
                        for k in range(4):
                            for e in range(2):
                                last = mm(PS[64 * e:64 * e + 64, 4 + n % 2, :], act_t[:, k, e * SLOTS:(e + 1) * SLOTS],
                                          w[e][:, k, :], start=k == 0, stop=k == 3, tile_position=(0, 64 * e))
                                if k == 3:
                                    last.then_inc(moe_out, 1)
                    pe.wait_ge(dn_copied, START + pair * 4 + 4)
                    pe.wait_ge(ct_copied, START + pair + 1)
                    for v in range(8):
                        pe.wait_ge(acc_done, START + it * 24 + (8 + 8 * p + v - 1))
                        for f in range(2):
                            last = mm(PS[:, 6 + v % 2, f * T:(f + 1) * T], yg[:, (2 * v + f) * P:(2 * v + f + 1) * P], cw_t)
                        last.then_inc(acc_mm, 1)

            with pe.Fori(0, 4) as g:
                group(g)
            with pe.If(nr > 1):
                with pe.Fori(1, nr) as r:
                    with pe.Fori(0, 4) as g:
                        group(r * 4 + g)
            for kt in range(KT):
                pe.wait_ge((sq3_ready, sq4_ready)[kt % 2], kt // 2 + 1)
                mm(PS[:, 5, 0:T], ones, sqn[:, kt % 2], start=kt == 0, stop=kt == KT - 1).then_inc(norm3_mm, 1)

        @block.scalar
        def _(act):
            for begun in (ada_copied, nar_act, silu_done, at_copied, dn_copied):
                act.sem_inc(begun, START)
            act.dma_start(par[:, :], params).then_inc(in_par, 16)
            act.dma_start(con[:, :], consts).then_inc(in_con, 16)
            act.dma_start(hl.rearrange("p k t -> p (k t)"), x_t).then_inc(in_x, 16)
            act.dma_start(hc.rearrange("p k t -> p (k t)"), ctx_t).then_inc(in_ctx, 16)
            act.dma_start(fin[0:64, :], filt_in).then_inc(in_filt, 16)
            act.dma_start(fw3[0:64, :], filt_w).then_inc(in_fw3, 16)
            act.dma_start(win.rearrange("p d n c -> p (d n c)"), windows).then_inc(in_win, 16)
            act.dma_start(lru_m[:, :, :].rearrange("p u m -> p (u m)"), lru_w).then_inc(in_lru, 16)
            f = act.activation
            step = Steps(act, act_main)

            act.wait_ge(in_par, 16)
            act.wait_ge(silu_zero, 1)
            f(silu_c[:, :, 0:2], par_("cond").rearrange("p (k b) -> p k b", b=2), ACT.Silu).then_inc(silu_ready, 1)
            def ada_copy(a, turn, slots):
                act.wait_ge(ring_out, used(turn, slots))
                act.wait_ge(ada_turned, START + a)
                f(arow[:, :], PS[:, 6, :], ACT.Copy).then_inc(ada_copied, 1)

            def filter_sin(i):
                act.wait_ge(arg_ready, i + 1)
                f(fh[0:64, :], fa[0:64, :], ACT.Sin).then_inc(sin_ready, 1)

            for a in range(ADA_FIRST):
                ada_copy(a, a // 2, 4 * (a % 2) + 4)
                if a in (0, 2):
                    filter_sin(a // 2)
                if a == 1:
                    act.wait_ge(in_con, 16)
                    act.wait_ge(norm_mm, KT)
                    f(rbc, PS[:, 5, :], ACT.Sqrt, bias=con_("eps"), scale=1.0 / D).then_inc(norm_root, 1)
                if a in (4, 6):
                    o = (a - 4) // 2
                    for u in range(4):
                        act.wait_ge(spec_mm, 4 * o + u + 1)
                        f(spec[:, u, o, :], PS[:, u, :], ACT.Copy).then_inc(spec_copied, 1)
                if a == 5:
                    act.wait_ge(lam_exp, 1)
                    f(small[:, 24:32], small[:, 16:24], ACT.Exp, scale=-1.0).then_inc(lam_exp, 1)
                if a == 6:
                    act.wait_ge(tnorm_mm, 1)
                    f(small[:, 0:8], PS[:, 4, 0:8], ACT.Sqrt, bias=con_("eps")).then_inc(tnorm_root, 1)
            for i in range(2):
                act.wait_ge(ring_out, used(T_WIDE + i, 4))
                act.wait_ge(tapsum_ready, 2)
                for c in (1, 3):
                    f(kvx[:, 4 * i + c, :, :], PS[:, c, :].rearrange("p (s t) -> p s t", s=2), ACT.Copy).then_inc(kv_act, 1)
                ada_copy(ADA_FIRST + i, T_WIDE + i, 8)
            def lru(c):
                if c:
                    act.wait_ge(lru_in, CT + c)
                for u in range(4):
                    act.wait_ge(lru_mm, 4 * c + u + 1)
                    d = u // 2
                    to, b = (lA[d], "lru_ba") if u % 2 == 0 else (lB[d], "lru_bx")
                    f(to, PS[:, 2 + u, :], ACT.Sigmoid, bias=par_(b, 4 * d + c, 4 * d + c + 1)).then_inc(lru_gate, 1)
                act.wait_ge(lam_ready, 1)
                act.wait_ge(lru_gate, 4 * c + 4)
                for d in range(2):
                    f(lT[d], lA[d], ACT.Tanh, scale=small[:, 32 + 4 * d + c:33 + 4 * d + c]).then_inc(act_main, 1)
                act.wait_ge(act_main, 2 * c + 2)
                for d in range(2):
                    f(lA[d], lA[d], ACT.Exp, scale=small[:, 40 + 4 * d + c:41 + 4 * d + c]).then_inc(lru_exp, 1)
                for d in range(2):
                    act.wait_ge(lru_var, 2 * c + d + 1)
                    f(lT[d], lT[d], ACT.Sqrt).then_inc(lru_root, 1)

            def p_exponent(u):
                h = u // 2
                act.wait_ge(sc_bias, u + 1)
                f(s_sb[u % 2], s_sb[u % 2], ACT.Exp, bias=small[:, 64 + u:65 + u], scale=HD ** -0.5,
                  accum_out=small[:, 80 + u:81 + u]).then_inc(p_exp, 1)
                f(small[:, 96 + u:97 + u], par_("sink", h, h + 1), ACT.Exp, bias=small[:, 64 + u:65 + u]).then_inc(p_exp, 1)

            def pt_copy(u):
                h, qt = u // 2, u % 2
                act.wait_ge(pt_mm, u + 1)
                if h >= 2:
                    act.wait_ge(pv_mm, h - 1)
                f(p_t[h % 2][:, :, qt * P:(qt + 1) * P], PS[:, 4, :].rearrange("p (k q) -> p k q", k=4),
                  ACT.Copy).then_inc(pt_copied, 1)

            def weave_mixers(slot):
                if slot in LRU_SLOTS:
                    lru(LRU_SLOTS.index(slot))
                if slot == Y_SLOT:
                    act.wait_ge(nar_dve, START + 3)
                    act.wait_ge(nar_act, START + 3)
                    f(proj[:, 8:12, :], proj[:, 8:12, :], ACT.Gelu_apprx_tanh).then_inc(gelu_ready, 1)
                u = slot - SCORE_SLOT
                if 1 <= u <= 16:
                    pt_copy(u - 1)
                if 0 <= u < 16:
                    p_exponent(u)

            for i in range(6):
                for q in range(4):
                    weave_mixers(5 * i + q)
                act.wait_ge(ring_out, used(T_NAR + i, 4))
                f(proj[:, 4 * i + 2:4 * i + 4, :], PS[:, 1, :].rearrange("p (s t) -> p s t", s=2), ACT.Copy).then_inc(nar_act, 1)
                ada_copy(A_NAR + i, T_NAR + i, 8)
                weave_mixers(5 * i + 4)

            def tokens_back(o):
                for nt in range(2):
                    act.wait_ge(hy_tmm, 2 * o + nt + 1)
                    f(ztok[:, nt, :], PS[:, 4 + nt, :], ACT.Copy).then_inc(hy_tcopied, 1)

            def gate(n, j, bank):
                act.wait_ge(ring_out, used(n * 3 + (T_MERGE + j // 2), 4 + 4 * (j % 2)))
                f(gates[j], PS[:, bank:bank + 2, :].rearrange("p a b -> p (a b)"), ACT.Sigmoid).then_inc(gate_sig, 1)

            def split(first, turn0, i):
                turn, slot, free = split_waits(i)
                act.wait_ge(ring_in[slot], (turn0 + (turn + 1)) * 16)
                act.wait_ge(ring_out, turn0 * RING + free)
                f(w_hi[i % 2], ring[:, slot], ACT.Copy).then_inc(split_hi, 1)

            def split_operand(to, x):
                f(to, x, ACT.Copy).then_inc(operand_hi, 1)

            act.wait_ge(pv_mm, 8)
            tokens_back(0)
            gate(0, 0, 0)
            tokens_back(1)
            gate(0, 1, 0)
            gate(0, 2, 0)
            act.wait_ge(mix_done, 1)
            split_operand(hl_hi, hl)
            ada_copy(A_MERGE, T_MERGE + 1, 8)
            for i in range(2):
                split(0, T_MERGE + 3, i)
            act.wait_ge(ring_out, used(T_MERGE + 2, 4))
            split_operand(mix_hi, proj[:, 0:12, :])
            split_operand(hv_hi, hv)
            ada_copy(A_MERGE + 1, T_MERGE + 2, 8)
            with act.Fori(1, 4) as n:
                turn0 = n * 3 + T_MERGE
                for i in range(2, 16):
                    split(n, turn0, i)
                    if i < 13 and i % 4 == 0:
                        act.wait_ge(br_used, n * 3 + (START - 3 + i // 4))
                        gate(n, i // 4 - 1, 2 * (i // 4 - 1))
                    if i == 13:
                        ada_copy(n * 2 + A_MERGE, n * 3 + (T_MERGE + 1), 8)
                for i in range(2):
                    split(n, turn0 + 3, i)
                ada_copy(n * 2 + (A_MERGE + 1), n * 3 + (T_MERGE + 2), 8)
            for q in range(4):
                if q == 3:
                    act.wait_ge(merged, 4)
                split_operand(m_hi[:, 4 * q:4 * q + 4, :], m_t[:, 4 * q:4 * q + 4, :])
            act.dma_start(x_res.rearrange("p k t -> p (k t)"), x_t).then_inc(in_res, 16)
            for i in range(2, 16):
                slot = i % RING
                act.wait_ge(ring_in[slot], (T_OUT + 1 + i // RING) * 16)
                act.wait_ge(ring_out, T_OUT * RING + i - 1)
                f(w_hi[i % 2], ring[:, slot], ACT.Copy).then_inc(split_hi, 1)
            act.wait_ge(norm2_mm, 1)
            f(rbn, PS[:, 5, 0:T], ACT.Sqrt, bias=con_("eps"), scale=1.0 / D).then_inc(norm2_root, 1)
            for kt in range(KT):
                act.wait_ge(fl_scaled, kt + 1)
                f(fl[:, kt, :], fl[:, kt, :], ACT.Identity, bias=mod[:, 3 * KT + kt, 0:1]).then_inc(fl_ready, 1)

            def tokens_copy(w):
                q, tt = w // 2, w % 2
                act.wait_ge(ft_mm, w + 1)
                f(fl_tok[:, tt, q * 512:(q + 1) * 512], PS[:, w % 4, :], ACT.Copy).then_inc(ft_copied, 1)

            act.wait_ge(router_mm, 1)
            f(rlog, PS[0:EXPERTS, 4, 0:T], ACT.Copy).then_inc(router_sb, 1)
            for w in range(4):
                tokens_copy(w)
            act.wait_ge(router_arg, 1)
            f(rt[:, 96:128], rt[:, 64:96], ACT.Exp).then_inc(router_exp, 1)
            for w in range(4, 8):
                tokens_copy(w)
            act.wait_ge(route_ready, 1)
            nr = act.value_load(rounds_i[0:1, 0:1], min_val=1, max_val=MAX_ROUNDS)

            def group(it):
                for p in range(2):
                    pair = it * 2 + p
                    c0 = it * (2 * PAIR_CHUNKS) + PAIR_CHUNKS * p
                    act.wait_ge(moe_out, c0 + 8)
                    act.wait_ge(act_ready, START + pair)
                    f(sg, PS[:, 0, :], ACT.Silu).then_inc(silu_done, 1)
                    act.wait_ge(at_mm, START + pair + 1)
                    f(act_t.rearrange("p k s -> p (k s)"), PS[:, 2, :], ACT.Copy).then_inc(at_copied, 1)
                    act.wait_ge(acc_mm, START + it * 24 + 16 * p)
                    for n in range(4):
                        act.wait_ge(moe_out, c0 + (16 + 2 * n + 2))
                        f(yg[:, n * 512:(n + 1) * 512], PS[:, 4 + n % 2, :], ACT.Copy).then_inc(dn_copied, 1)

            with act.Fori(0, 4) as g:
                group(g)
            with act.If(nr > 1):
                with act.Fori(1, nr) as r:
                    with act.Fori(0, 4) as g:
                        group(r * 4 + g)
            act.wait_ge(y_ready, 1)
            for kt in range(0, KT, 2):
                if kt:
                    act.wait_ge(norm3_mm, kt - 1)
                f(sqn[:, 0], x_res[:, kt, :], ACT.Square).then_inc(sq3_ready, 1)
            act.wait_ge(norm3_mm, KT)
            f(rbn, PS[:, 5, 0:T], ACT.Sqrt, bias=con_("eps"), scale=1.0 / D).then_inc(norm3_root, 1)

        @block.vector
        def _(dve):
            for begun in (ada_added, nar_dve, br_used, out_used, acc_done, act_ready, ct_copied):
                dve.sem_inc(begun, START)
            v = nc.vector
            step = Steps(dve, dve_main)

            dve.memset(silu_c[:, :, :], 0.0).then_inc(silu_zero, 1)
            dve.wait_ge(in_par, 16)
            def ada_add(a):
                dve.wait_ge(ada_turned, START + a + 1)
                lo = PARAM_AT["b_ada"][0]
                sums = PS[:, 7, :].rearrange("p (c j r) -> p c r j", c=4, j=4)[:, :, 0:2, :]
                dve.tensor_reduce(ada_sum.rearrange("p (c r) -> p c r", c=4), sums, AX.X, ALU.add).then_inc(ada_summed, 1)
                dve.wait_ge(ada_summed, a + 1)
                dve.tensor_tensor(mod[:, bass.ds(a * 4, 4), :].rearrange("p k b -> p (k b)"), ada_sum,
                                  par[:, bass.ds(a * 8 + lo, 8)], ALU.add).then_inc(ada_added, 1)

            def squares():
                dve.wait_ge(in_con, 16)
                dve.wait_ge(in_x, 16)
                dve.wait_ge(in_ctx, 16)
                for kt in range(KT):
                    if kt >= 2:
                        dve.wait_ge(norm_mm, kt - 1)
                    dve.tensor_tensor(sq[:, kt % 2].rearrange("p (s t) -> p s t", s=2), norm_x[:, :, kt, :],
                                      norm_x[:, :, kt, :], ALU.mult).then_inc(sq_ready, 1)

            def reduced(i, bank, bias):
                a, k = fa[0:64, :], fk[0:64, :]
                dve.wait_ge(arg_mm, i + 1)
                if i:
                    dve.wait_ge(sin_ready, i)
                step.done(dve.tensor_scalar(a, PS[0:64, bank, 0:T], par_(bias)[0:64], par_("freq")[0:64], ALU.add, ALU.mult))
                step.done(dve.tensor_scalar(k, a, 1.0 / TWO_PI, ROUND_MAGIC, ALU.mult, ALU.add))
                step.done(dve.tensor_scalar(k, k, -ROUND_MAGIC, None, ALU.add))
                for part in TWO_PI_PARTS:
                    step.done(dve.scalar_tensor_tensor(out=a, in0=k, scalar=-part, in1=a, op0=ALU.mult, op1=ALU.add))
                dve.tensor_scalar(a, a, 3.1415925, -3.1415925, ALU.min, ALU.max).then_inc(arg_ready, 1)

            def normalise_streams():
                for kt in range(KT):
                    for s in range(2):
                        last = dve.tensor_tensor(norm_x[:, s, kt, :], norm_x[:, s, kt, :], rbc[:, s * T:(s + 1) * T], ALU.mult)
                last.then_inc(norm_ready, 1)

            def filter_windowed(o):
                if o == 0:
                    dve.wait_ge(in_win, 16)
                for u in range(4):
                    nt, d = u // 2, u % 2
                    dve.wait_ge(tap_mm, 4 * o + u + 1)
                    last = dve.tensor_tensor(taps[:, nt, d, :], PS[:, u, :], win[:, d, nt, :], ALU.mult)
                step.done(last)
                dve.tensor_tensor(tsq[:, :, :, :], taps[:, :, :, :], taps[:, :, :, :], ALU.mult)
                if o:
                    dve.wait_ge(spec_mm, 4)
                step.done(dve.tensor_tensor(tapsum[:, :, 0, :], taps[:, :, 0, :], taps[:, :, 1, :], ALU.add))
                step.done(dve.tensor_tensor(tsum[:, o, :], tsq[:, 0, 0, :], tsq[:, 0, 1, :], ALU.add))
                step.done(dve.tensor_tensor(tsum[:, o, :], tsum[:, o, :], tsq[:, 1, 0, :], ALU.add))
                step.done(dve.tensor_tensor(tsum[:, o, :], tsum[:, o, :], tsq[:, 1, 1, :], ALU.add))
                dve.tensor_tensor(tapsum[:, :, 1, :], taps[:, :, 0, :], taps[:, :, 1, :], ALU.subtract).then_inc(tapsum_ready, 1)

            z, az, u_, s_, s2, pol, c8, nc8 = (small[:, a:a + 8] for a in (112, 16, 24, 120, 128, 136, 32, 40))
            step.done(dve.tensor_scalar(z, par_("lam"), -1.0, None, ALU.mult))
            step.done(dve.tensor_tensor(az, par_("lam"), z, ALU.max))
            dve.tensor_scalar(small[:, 56:64], par_("sink"), -1.0, None, ALU.mult).then_inc(lam_exp, 1)

            for a in range(ADA_FIRST):
                ada_add(a)
                if a == 0:
                    reduced(0, 4, "fb1")
                if a == 1:
                    squares()
                    dve.wait_ge(norm_root, 1)
                    step.done(dve.reciprocal(rbc, rbc))
                if a == 2:
                    reduced(1, 3, "fb2")
                    normalise_streams()
                if a in (3, 5):
                    filter_windowed((a - 3) // 2)
                if a == 6:
                    dve.wait_ge(tnorm_root, 1)
                    step.done(dve.reciprocal(small[:, 8:16], small[:, 0:8]))
            dve.wait_ge(ada_added, START + ADA_FIRST)
            dve.wait_ge(norm_ready, 1)

            def scale_gain(first, gain, cols):
                step.done(dve.tensor_scalar(modA[:, :, 0:cols], mod[:, first:first + KT, 0:cols], 1.0, None, ALU.add))
                g = par_(gain).rearrange("p (k b) -> p k b", b=2 if cols == 2 else 1)
                step.done(dve.tensor_tensor(modA[:, :, 0:cols], modA[:, :, 0:cols], g, ALU.mult))

            scale_gain(KT, "g_mix", 2)
            for kt in range(KT):
                for s, b in ((0, 1), (1, 0)):
                    last = dve.tensor_scalar(norm_x[:, s, kt, :], norm_x[:, s, kt, :], modA[:, kt, b:b + 1],
                                             mod[:, kt, b:b + 1], ALU.mult, ALU.add)
                last.then_inc(h_ready, 1)
            dve.wait_ge(lam_exp, 2)
            step.done(dve.tensor_scalar(s_, u_, 2.0, None, ALU.add))
            step.done(dve.reciprocal(s_, s_))
            step.done(dve.tensor_tensor(s_, s_, u_, ALU.mult))
            step.done(dve.tensor_tensor(s2, s_, s_, ALU.mult))
            step.done(dve.tensor_scalar(pol, s2, 1.0 / 19, 1.0 / 17, ALU.mult, ALU.add))
            for k in range(7, -1, -1):
                step.done(dve.tensor_tensor(pol, pol, s2, ALU.mult))
                step.done(dve.tensor_scalar(pol, pol, 1.0 / (2 * k + 1), None, ALU.add))
            step.done(dve.tensor_tensor(pol, pol, s_, ALU.mult))
            step.done(dve.tensor_scalar(z, z, 0.0, None, ALU.max))
            step.done(dve.scalar_tensor_tensor(out=z, in0=pol, scalar=2.0, in1=z, op0=ALU.mult, op1=ALU.add))
            dve.tensor_scalar(c8, z, 8.0, None, ALU.mult).then_inc(lam_ready, 1)
            step.done(dve.tensor_scalar(nc8, z, -8.0, None, ALU.mult))
            for i in range(2):
                dve.wait_ge(ring_out, used(T_WIDE + i, 4))
                for c in (0, 2):
                    dve.tensor_copy(kvx[:, 4 * i + c, :, :], PS[:, c, :].rearrange("p (s t) -> p s t", s=2)).then_inc(kv_dve, 1)
                ada_add(ADA_FIRST + i)
            dve.wait_ge(kv_dve, 4)
            dve.wait_ge(kv_act, 4)
            for c in range(CT):
                x, y = kvx[:, 4 + c, :, :], xc[:, c, :].rearrange("p (s t) -> p s t", s=2)
                w = lambda j: par_("lru_w", 4 * j + c, 4 * j + c + 1)
                step.done(dve.tensor_scalar(y, x, w(2), par_("lru_b", c, c + 1), ALU.mult, ALU.add))
                step.done(dve.scalar_tensor_tensor(out=y[:, :, 2:T], in0=x[:, :, 0:T - 2], scalar=w(0), in1=y[:, :, 2:T], op0=ALU.mult, op1=ALU.add))
                step.done(dve.scalar_tensor_tensor(out=y[:, :, 1:T], in0=x[:, :, 0:T - 1], scalar=w(1), in1=y[:, :, 1:T], op0=ALU.mult, op1=ALU.add))
                dve.scalar_tensor_tensor(out=y[:, :, 0:T - 1], in0=x[:, :, 1:T], scalar=w(3), in1=y[:, :, 0:T - 1], op0=ALU.mult, op1=ALU.add).then_inc(lru_in, 1)

            def lru(c):
                if c == 0:
                    dve.wait_ge(lru_in, CT)
                for d in range(2):
                    dve.wait_ge(lru_exp, 2 * c + d + 1)
                    dve.tensor_tensor(lB[d], lB[d], xc[:, c, :], ALU.mult)
                    step.done(dve.tensor_tensor(lU, lA[d], lA[d], ALU.mult))
                    dve.scalar_tensor_tensor(out=lT[d], in0=lU, scalar=1.0, in1=lT[d], op0=ALU.add, op1=ALU.mult).then_inc(lru_var, 1)
                    dve.wait_ge(lru_var, 2 * c + d + 1)
                for d in range(2):
                    dve.wait_ge(lru_root, 2 * c + d + 1)
                    step.done(dve.tensor_tensor(lB[d], lB[d], lT[d], ALU.mult))
                    if d == 0:
                        step.done(dve.tensor_tensor_scan(lT[0], lA[0], lB[0], 0.0, ALU.mult, ALU.add))
                    else:
                        for s in range(2):
                            o_, a_, b_ = (t[:, s * T:(s + 1) * T][:, ::-1] for t in (lT[1], lA[1], lB[1]))
                            step.done(dve.tensor_tensor_scan(o_, a_, b_, 0.0 if s == 0 else lT[1][:, 0:1], ALU.mult, ALU.add))
                dve.tensor_tensor(xc[:, c, 0:T], lT[0][:, T:2 * T], lT[1][:, T:2 * T], ALU.add).then_inc(lru_in, 1)
                dve.wait_ge(lru_in, CT + c + 1)

            def rotate(u):
                dve.wait_ge(rot_mm, u + 1)
                src = kvx[:, 0:2, 1, :] if u == 0 else proj[:, 2 * u - 2:2 * u, :]
                for h in range(2):
                    dve.tensor_tensor(rtmp[:, h * T:(h + 1) * T], PS[:, 4 + u % 2, h * T:(h + 1) * T], rope[:, 1, :], ALU.mult)
                    last = dve.tensor_tensor(src[:, h, :], src[:, h, :], rope[:, 0, :], ALU.mult)
                step.done(last)
                last = dve.tensor_tensor(src, src, rtmp.rearrange("p (s t) -> p s t", s=2), ALU.add)
                last.then_inc(rot_used, 1)
                dve.wait_ge(rot_used, u + 1)

            def row_max(u):
                h, qt = u // 2, u % 2
                dve.wait_ge(sc_mm, u + 1)
                if u >= 2:
                    dve.wait_ge(pt_mm, u - 1)
                dve.tensor_tensor_reduce(s_sb[u % 2], PS[:, 2 + u % 2, :], mask[:, qt, :], 1.0, NEG, ALU.add, ALU.max,
                                         small[:, 144 + u:145 + u]).then_inc(sc_read, 1)
                dve.wait_ge(sc_read, u + 1)
                dve.tensor_scalar(small[:, 64 + u:65 + u], small[:, 144 + u:145 + u], -(HD ** -0.5), small[:, 56 + h:57 + h],
                                  ALU.mult, ALU.min).then_inc(sc_bias, 1)

            def normalise(u):
                dve.wait_ge(p_exp, 2 * u + 2)
                den = small[:, 160 + u:161 + u]
                step.done(dve.tensor_tensor(den, small[:, 80 + u:81 + u], small[:, 96 + u:97 + u], ALU.add))
                step.done(dve.reciprocal(den, den))
                dve.tensor_scalar(s_sb[u % 2], s_sb[u % 2], den, None, ALU.mult).then_inc(p_ready, 1)

            def pv_copy(h):
                dve.wait_ge(pv_mm, h + 1)
                dve.tensor_copy(proj[:, h, :], PS[:, 5, 0:T]).then_inc(pv_copied, 1)

            def short_conv(src, dst, wi):
                w = lambda j: par_("hy_w", 12 * j + wi, 12 * j + wi + 1)
                step.done(dve.tensor_scalar(dst, src, w(1), par_("hy_b", wi, wi + 1), ALU.mult, ALU.add))
                step.done(dve.scalar_tensor_tensor(out=dst[:, 1:T], in0=src[:, 0:T - 1], scalar=w(0), in1=dst[:, 1:T], op0=ALU.mult, op1=ALU.add))
                return dve.scalar_tensor_tensor(out=dst[:, 0:T - 1], in0=src[:, 1:T], scalar=w(2), in1=dst[:, 0:T - 1], op0=ALU.mult, op1=ALU.add)

            def projected(panels):
                dve.wait_ge(nar_dve, START + panels)
                dve.wait_ge(nar_act, START + panels)

            def weave_mixers(slot):
                if slot in LRU_SLOTS:
                    lru(LRU_SLOTS.index(slot))
                for u in ROTATE_SLOTS.get(slot, ()):
                    rotate(u)
                if slot == VALUE_SLOT:
                    dve.wait_ge(vt_mm, 1)
                    dve.tensor_copy(v_tok.rearrange("p k c -> p (k c)"), PS[:, 4:6, :].rearrange("p a b -> p (a b)")).then_inc(vt_copied, 1)
                u = slot - SCORE_SLOT
                if 0 <= u < 16:
                    row_max(u)
                if u >= 3 and u % 2 == 1 and u <= 17:
                    pv_copy((u - 3) // 2)
                if 0 <= u < 16:
                    normalise(u)
                if slot == Y_SLOT + 1:
                    dve.wait_ge(gelu_ready, 1)
                    last = dve.tensor_tensor(proj[:, 8:12, :], proj[:, 8:12, :], xc[:, :, 0:T], ALU.mult)
                    last.then_inc(lru_done, 1)
                    dve.wait_ge(lru_done, 1)
                if 20 <= slot < 24:
                    projected(4)
                    c = slot - 20
                    ins = short_conv(proj[:, 12 + c, :], hv[:, c, :], c)
                    if c < 3:
                        step.done(ins)
                    else:
                        ins.then_inc(hy_in, 1)
                        dve.wait_ge(hy_in, 1)
                if 25 <= slot < 29:
                    projected(5)
                    c = slot - 25
                    step.done(short_conv(proj[:, 16 + c, :], proj[:, 12 + c, :], 4 + c))

            for i in range(6):
                for q in range(4):
                    weave_mixers(5 * i + q)
                dve.wait_ge(ring_out, used(T_NAR + i, 4))
                dve.tensor_copy(proj[:, 4 * i:4 * i + 2, :], PS[:, 0, :].rearrange("p (s t) -> p s t", s=2)).then_inc(nar_dve, 1)
                ada_add(A_NAR + i)
                weave_mixers(5 * i + 4)
            projected(6)
            for c in range(CT):
                step.done(short_conv(proj[:, 20 + c, :], proj[:, 16 + c, :], 8 + c))

            for o in range(2):
                for kk in range(2):
                    dve.wait_ge(hy_fmm, 4 * o + 2 * kk + 2)
                    zr, zs = PS[:, 2 + 2 * kk, :], PS[:, 3 + 2 * kk, :]
                    hr, hs = spec[:, kk, o, :], spec[:, 2 + kk, o, :]
                    dve.tensor_tensor(ht[0], zr, hr, ALU.mult)
                    step.done(dve.tensor_tensor(ht[1], zs, hs, ALU.mult))
                    step.done(dve.tensor_tensor(ysp[:, kk, :], ht[0], ht[1], ALU.subtract))
                    dve.tensor_tensor(ht[0], zr, hs, ALU.mult)
                    step.done(dve.tensor_tensor(ht[1], zs, hr, ALU.mult))
                    last = dve.tensor_tensor(ysp[:, 2 + kk, :], ht[0], ht[1], ALU.add)
                    if kk == 0:
                        step.done(last)
                last.then_inc(hy_ready, 1)
                for c in range(CT):
                    dve.wait_ge(hy_imm, 4 * o + 2 * (c // 2) + 2)
                    z = hv[:, c, :]
                    t = ht[c % 2][:, 0:T]
                    step.done(dve.tensor_scalar(t, PS[:, 2 + c // 2, (c % 2) * T:(c % 2 + 1) * T], small[:, 8 + 4 * o + c:9 + 4 * o + c], None, ALU.mult))
                    step.done(dve.scalar_tensor_tensor(out=z, in0=z, scalar=par_("skip", 4 * o + c, 4 * o + c + 1), in1=t, op0=ALU.mult, op1=ALU.add))
                    ins = dve.tensor_tensor(z, z, proj[:, 12 + 4 * o + c, :], ALU.mult)
                    if c < 3:
                        step.done(ins)
                    elif o == 0:
                        ins.then_inc(hy_in, 1)
                        dve.wait_ge(hy_in, 2)
                    else:
                        ins.then_inc(mix_done, 1)

            def split(count, i, slot):
                dve.wait_ge(split_hi, count + 1)
                dve.tensor_tensor(ring_r[:, slot], ring[:, slot], w_hi[i % 2], ALU.subtract).then_inc(split_lo, 1)

            def split_operand(count, low, x, high):
                dve.wait_ge(operand_hi, count)
                dve.tensor_tensor(low, x, high, ALU.subtract).then_inc(operand_lo, 1)

            def merge(n, j):
                m = m_t[:, bass.ds(n * 4, 4), :].rearrange("p k t -> p (k t)")
                dve.wait_ge(gate_sig, n * 3 + (j + 1))
                dve.wait_ge(ring_out, used(n * 3 + (T_MERGE + 2), 2 + j))
                src = PS[:, 2 * j:2 * j + 2, :].rearrange("p a b -> p (a b)")
                dve.tensor_tensor(m if j == 0 else gtmp, src, gates[j], ALU.mult).then_inc(br_used, 1)
                dve.wait_ge(br_used, START + n * 3 + (j + 1))
                if j:
                    ins = dve.tensor_tensor(m, m, gtmp, ALU.add)
                    if j == 1:
                        ins.then_inc(summed, 1)
                        dve.wait_ge(summed, n + 1)
                    else:
                        ins.then_inc(merged, 1)
                        dve.wait_ge(merged, n + 1)

            split_operand(1, hl_lo, hl, hl_hi)
            ada_add(A_MERGE)
            merge(0, 0)
            split(0, 0, 0)
            merge(0, 1)
            split(1, 1, 1)
            merge(0, 2)
            split_operand(2, mix_lo, proj[:, 0:12, :], mix_hi)
            split_operand(3, hv_lo, hv, hv_hi)
            ada_add(A_MERGE + 1)
            with dve.Fori(1, 4) as n:
                first = (n - 1) * 16
                for i in range(2, 16):
                    split(first + i, i, split_waits(i)[1])
                    if i == 13:
                        ada_add(n * 2 + A_MERGE)
                merge(n, 0)
                split(first + 16, 0, 0)
                merge(n, 1)
                split(first + 17, 1, 1)
                merge(n, 2)
                ada_add(n * 2 + (A_MERGE + 1))
            for q in range(4):
                split_operand(4 + q, *(b[:, 4 * q:4 * q + 4, :] for b in (m_lo, m_t, m_hi)))

            dve.wait_ge(ada_added, START + ADA_PANELS)
            for p in range(4):
                for i in range(4 * p + 2, min(4 * p + 6, 16)):
                    split(48 + i, i, i % RING)
                if p == 0:
                    step.done(dve.memset(sqsum, 0.0))
                    dve.wait_ge(in_res, 16)
                dve.wait_ge(ring_out, used(T_OUT, 4 * p + 4))
                for c in range(4):
                    kt = 4 * p + c
                    x = x_res[:, kt, :]
                    step.done(dve.scalar_tensor_tensor(out=x, in0=PS[:, 2 * (p % 2) + c // 2, (c % 2) * T:(c % 2 + 1) * T],
                                                       scalar=mod[:, 2 * KT + kt, 0:1], in1=x, op0=ALU.mult, op1=ALU.add))
                    if c == 3:
                        dve.tensor_copy(small[:, 176:177], small[:, 8:9]).then_inc(out_used, 1)
                    step.done(dve.tensor_tensor(sqn[:, 0], x, x, ALU.mult))
                    step.done(dve.tensor_tensor(sqsum, sqsum, sqn[:, 0], ALU.add))
            dve.wait_ge(out_used, START + 4)
            dve.tensor_copy(small[:, 177:178], small[:, 8:9]).then_inc(sq2_ready, 1)
            step.done(dve.tensor_scalar(modA[:, :, 0], mod[:, 4 * KT:5 * KT, 0], 1.0, None, ALU.add))
            step.done(dve.tensor_tensor(modA[:, :, 0], modA[:, :, 0], par_("g_ffn"), ALU.mult))
            dve.wait_ge(norm2_root, 1)
            step.done(dve.reciprocal(rbn, rbn))
            for kt in range(KT):
                dve.scalar_tensor_tensor(out=fl[:, kt, :], in0=x_res[:, kt, :], scalar=modA[:, kt, 0:1], in1=rbn,
                                         op0=ALU.mult, op1=ALU.mult).then_inc(fl_scaled, 1)

            t3 = lambda a, n=16: rt[:, a:a + 2 * n].rearrange("p (t e) -> p t e", t=2)
            choice, logit, shifted, prob, pick1, pick2, tmp, eq, wsum = (
                t3(0), t3(32), t3(64), t3(96), t3(128), t3(160), t3(192), t3(224), t3(256))
            gm, gq = t3(288, 4), t3(296, 4)
            col = lambda k: small[:, 180 + 2 * k:182 + 2 * k]
            c3 = lambda k: col(k).unsqueeze(2)
            dve.wait_ge(router_turned, 1)
            for tt in range(2):
                last = dve.tensor_tensor(logit[:, tt, :], PS[:, 5, 64 + tt * 16:80 + tt * 16], par_("router_b"), ALU.add)
            step.done(last)
            step.done(dve.tensor_reduce(col(0), logit, AX.X, ALU.max))
            for tt in range(2):
                last = dve.tensor_scalar(shifted[:, tt, :], logit[:, tt, :], col(0)[:, tt:tt + 1], None, ALU.subtract)
            last.then_inc(router_arg, 1)
            dve.wait_ge(router_exp, 1)
            step.done(dve.tensor_reduce(col(1), prob, AX.X, ALU.add))
            step.done(dve.reciprocal(col(1), col(1)))
            for tt in range(2):
                last = dve.tensor_scalar(prob[:, tt, :], prob[:, tt, :], col(1)[:, tt:tt + 1], None, ALU.mult)
            step.done(last)

            def first_max(values, out_, scratch, down, top):
                step.done(dve.tensor_reduce(top, values, AX.X, ALU.max))
                for tt in range(2):
                    last = dve.scalar_tensor_tensor(out=scratch[:, tt, :], in0=values[:, tt, :], scalar=top[:, tt:tt + 1],
                                                    in1=down, op0=ALU.is_equal, op1=ALU.mult)
                step.done(last)
                step.done(dve.tensor_reduce(col(7), scratch, AX.X, ALU.max))
                for tt in range(2):
                    last = dve.tensor_scalar(out_[:, tt, :], scratch[:, tt, :], col(7)[:, tt:tt + 1], None, ALU.is_equal)
                step.done(last)

            step.done(dve.tensor_reduce(gm.rearrange("p t g -> p (t g)"), rt[:, 96:128].rearrange("p (g e) -> p g e", e=4), AX.X, ALU.max))
            first_max(gm, gq, t3(304, 4), con_("down4"), col(2))
            for g in range(8):
                a = g * 4
                last = dve.tensor_scalar(rt[:, 192 + a:196 + a], rt[:, 96 + a:100 + a], rt[:, 296 + g:297 + g], None, ALU.mult)
            step.done(last)
            step.done(dve.tensor_scalar(rt[:, 296:304], rt[:, 296:304], -1.0, None, ALU.add))
            for g in range(8):
                a = g * 4
                last = dve.tensor_scalar(rt[:, 192 + a:196 + a], rt[:, 192 + a:196 + a], rt[:, 296 + g:297 + g], None, ALU.add)
            step.done(last)
            first_max(tmp, pick1, eq, con_("down16"), col(3))
            step.done(dve.scalar_tensor_tensor(out=rt[:, 192:224], in0=rt[:, 128:160], scalar=-4.0, in1=rt[:, 192:224], op0=ALU.mult, op1=ALU.add))
            first_max(tmp, pick2, eq, con_("down16"), col(4))
            dve.tensor_tensor(rt[:, 0:32], rt[:, 128:160], rt[:, 160:192], ALU.add).then_inc(pick_ready, 1)
            step.done(dve.tensor_tensor(col(5), col(3), col(4), ALU.add))
            step.done(dve.reciprocal(col(5), col(5)))
            for tt in range(2):
                dve.tensor_scalar(pick1[:, tt, :], pick1[:, tt, :], col(3)[:, tt:tt + 1], col(5)[:, tt:tt + 1], ALU.mult, ALU.mult)
                last = dve.tensor_scalar(pick2[:, tt, :], pick2[:, tt, :], col(4)[:, tt:tt + 1], col(5)[:, tt:tt + 1], ALU.mult, ALU.mult)
            step.done(last)
            step.done(dve.tensor_tensor(weight, rt[:, 128:160], rt[:, 160:192], ALU.add))
            dve.wait_ge(rank_mm, 1)
            dve.wait_ge(pick_ready, 1)
            step.done(dve.scalar_tensor_tensor(out=rank, in0=PS[:, 5, 0:32], scalar=1.0, in1=rt[:, 0:32], op0=ALU.add, op1=ALU.mult))
            step.done(dve.tensor_scalar(rank, rank, -1.0, None, ALU.add))
            step.done(dve.tensor_reduce(small[:, 200:201], PS[:, 5, 32:48], AX.X, ALU.max))
            for k in range(1, MAX_ROUNDS):
                step.done(dve.tensor_scalar(small[:, 200 + k:201 + k], small[:, 200:201], float(k * SLOTS), None, ALU.is_gt))
            step.done(dve.memset(small[:, 200:201], 1.0))
            step.done(dve.tensor_reduce(small[:, 204:205], small[:, 200:204], AX.X, ALU.add))
            dve.tensor_copy(rounds_i[:, :], small[0:1, 204:205]).then_inc(route_ready, 1)
            dve.wait_ge(route_ready, 1)
            nr = dve.value_load(rounds_i[0:1, 0:1], min_val=1, max_val=MAX_ROUNDS)

            def group(it, g):
                for tt in range(2):
                    for e in range(4):
                        r_ = rank[:, bass.ds(g * 4 + (16 * tt + e), 1)]
                        w_ = weight[:, bass.ds(g * 4 + (16 * tt + e), 1)]
                        dve.tensor_scalar(disp[:, tt, e * SLOTS:(e + 1) * SLOTS], con_("iota"), r_, None, ALU.is_equal)
                        last = dve.tensor_scalar(comb[:, tt, e * SLOTS:(e + 1) * SLOTS], con_("iota"), r_, w_, ALU.is_equal, ALU.mult)
                last.then_inc(disp_ready, 1)
                dve.wait_ge(disp_ready, it + 1)
                for tt in range(2):
                    r_ = rank[:, bass.ds(g * 4 + 16 * tt, 4)]
                    dve.tensor_scalar(r_, r_, -float(SLOTS), None, ALU.add).then_inc(dve_moe, 1)
                dve.wait_ge(dve_moe, it * 2 + 2)
                for v_ in range(8):
                    dve.wait_ge(acc_mm, START + it * 24 + (v_ + 1))
                    dve.tensor_copy(xg[:, 2 * v_:2 * v_ + 2, :], PS[:, 6 + v_ % 2, :].rearrange("p (f t) -> p f t", f=2)).then_inc(acc_done, 1)
                for p in range(2):
                    pair = it * 2 + p
                    dve.wait_ge(ct_mm, pair + 1)
                    dve.tensor_copy(cw_t, PS[:, 3, 0:T]).then_inc(ct_copied, 1)
                    dve.wait_ge(silu_done, START + pair + 1)
                    dve.wait_ge(moe_out, it * (2 * PAIR_CHUNKS) + (PAIR_CHUNKS * p + 16))
                    dve.wait_ge(at_mm, START + pair)
                    dve.tensor_tensor(act_sb, PS[:, 1, :], sg, ALU.mult).then_inc(act_ready, 1)
                    for v_ in range(8):
                        dve.wait_ge(acc_mm, START + it * 24 + (8 + 8 * p + v_ + 1))
                        for f in range(2):
                            x = x_res[:, 2 * v_ + f, :]
                            last = dve.scalar_tensor_tensor(out=x, in0=PS[:, 6 + v_ % 2, f * T:(f + 1) * T],
                                                            scalar=mod[:, 5 * KT + 2 * v_ + f, 0:1], in1=x, op0=ALU.mult, op1=ALU.add)
                        last.then_inc(acc_done, 1)

            with dve.Fori(0, 4) as g:
                group(g, g)
            with dve.If(nr > 1):
                with dve.Fori(1, nr) as r:
                    with dve.Fori(0, 4) as g:
                        group(r * 4 + g, g)

            end = Steps(dve, dve_end)
            dve.memset(small[:, 210:211], 0.0).then_inc(y_ready, 1)
            dve.wait_ge(y_ready, 1)
            for kt in range(1, KT, 2):
                if kt > 1:
                    dve.wait_ge(norm3_mm, kt - 1)
                dve.tensor_tensor(sqn[:, 1], x_res[:, kt, :], x_res[:, kt, :], ALU.mult).then_inc(sq4_ready, 1)
            dve.wait_ge(norm3_root, 1)
            end.done(dve.reciprocal(rbn, rbn))
            for kt in range(KT):
                last = dve.scalar_tensor_tensor(out=x_res[:, kt, :], in0=x_res[:, kt, :], scalar=par_("final_g", kt, kt + 1),
                                                in1=rbn, op0=ALU.mult, op1=ALU.mult)
                if kt % 4 == 3:
                    last.then_inc(out_ready, 1)


def _constants():
    f = np.float32
    con = np.zeros((P, CONST_N), f)

    def put(name, a):
        lo, hi = CONST_AT[name]
        con[:, lo:hi] = np.broadcast_to(np.asarray(a, f).reshape(-1, hi - lo), (P, hi - lo))

    p = np.arange(P)
    put("ident", np.eye(P))
    put("ones", np.ones((P, P)))
    put("before", p[:, None] < p[None, :])
    rot = np.zeros((P, P))
    rot[p[:64] + 64, p[:64]] = -1.0
    rot[p[:64], p[:64] + 64] = 1.0
    put("rot", rot)
    put("iota", np.arange(SLOTS))
    sel = np.zeros((P, 2))
    for j in range(4):
        sel[32 * j, 0] = sel[32 * j + 1, 1] = 1.0
    put("sel", sel)
    put("eps", np.full((1, 1), EPS))
    put("down16", EXPERTS - np.arange(EXPERTS))
    put("down4", GROUPS - np.arange(GROUPS))
    tok = np.arange(T)
    inv = (f(10000.0) ** (-np.arange(32, dtype=f) / f(32))).astype(f)
    ang = np.concatenate([(tok // GRID_W).astype(f)[:, None] * inv, (tok % GRID_W).astype(f)[:, None] * inv], 1)
    ang = np.concatenate([ang, ang], 1).T
    put("rope", np.concatenate([np.cos(ang), np.sin(ang)], 1))
    mask = np.zeros((P, 2, 512))
    for qt in range(2):
        qi = qt * P + p
        mask[:, qt, T:] = np.where(np.abs(qi[:, None] - tok[None, :]) <= WINDOW, 0.0, NEG)
    put("mask", mask.reshape(P, -1))
    theta = (2.0 * np.arange(T) + 1.0) * np.pi / (2 * T)
    n = np.arange(T)
    cs = np.concatenate([np.cos(n[:, None] * theta), np.sin(n[:, None] * theta)], 1)
    put("dft", cs.reshape(2, P, 2 * T).transpose(1, 0, 2).reshape(P, -1))
    back = np.concatenate([np.cos(theta[:, None] * n), np.sin(theta[:, None] * n)], 0) / T
    put("idft", back.reshape(4, P, T).transpose(1, 0, 2).reshape(P, -1))

    t = np.linspace(0.0, 1.0, T, dtype=f)[:, None]
    w = (f(TWO_PI) * np.arange(T, dtype=f)[:, None] / f(T)).astype(f)
    bands = np.linspace(1e-4, BANDS - 1, BANDS, dtype=f)[None, :]
    z = np.concatenate([t, np.cos(bands * w), -np.sin(bands * w)], 1).T
    deltas = np.abs(np.linspace(np.log(1e-2) / 0.3, np.log(1e-2) / 1.5, HY, dtype=f))
    win = np.exp(-t * deltas[None, :]).astype(f)
    back_win = win.copy()
    back_win[0] = 0.0
    windows = np.stack([win, back_win]).reshape(2, 2, P, HY).transpose(2, 0, 1, 3).reshape(P, -1)
    return con, z.astype(f), np.ascontiguousarray(windows)


def _panels(w):
    k, n = w.shape
    return w.reshape(k // 512, 4, P, n // 512, 512).transpose(3, 0, 2, 1, 4).reshape(-1, P, CHUNK)


IN_ORDER = [0, 1, 2, 3, 7, 4, 5, 6] + list(range(8, 20))


def _cols(v):
    v = np.asarray(v)
    return v.reshape(-1, P).T


def kernel(**inputs):
    from concourse import bacc
    from concourse.bass_utils import run_bass_kernel_spmd

    a = {k: np.asarray(v) for k, v in inputs.items()}
    consts, z, windows = _constants()
    par = np.zeros((P, PARAM_N), np.float32)

    def put(name, x):
        lo, hi = PARAM_AT[name]
        par[:, lo:hi] = x

    def put64(name, x):
        lo, hi = PARAM_AT[name]
        par[:FILTER_HIDDEN, lo:hi] = x.reshape(FILTER_HIDDEN, 1)

    put("cond", np.stack([_cols(a["c"][0]), _cols(a["c_ctx"])], 2).reshape(P, -1))
    put("b_ada", np.repeat(_cols(a["b_ada"][0]), 2, axis=1))
    put("g_mix", np.repeat(_cols(a["g_mix"][0]), 2, axis=1))
    put("g_ffn", _cols(a["g_ffn"][0]))
    put("final_g", _cols(a["final_g"]))
    put("sink", np.broadcast_to(a["attn_sink"][0], (P, HEADS)))
    put("hy_w", _cols(a["hy_short_w"][0]))
    put("hy_b", _cols(a["hy_short_b"][0]))
    put("skip", _cols(a["hy_skip"][0]))
    put("lru_w", _cols(a["lru_conv_w"][0]))
    put("lru_b", _cols(a["lru_conv_b"][0]))
    put("lru_ba", _cols(a["lru_ba"][0]))
    put("lru_bx", _cols(a["lru_bx"][0]))
    put("lam", _cols(a["lru_lambda"][0]))
    put64("freq", a["hy_freq"][0])
    put64("fb1", a["hy_b1"][0])
    put64("fb2", a["hy_b2"][0])
    put("router_b", np.broadcast_to(a["router_b"], (P, EXPERTS)))
    put("router_w", a["router_w"].reshape(KT, P, EXPERTS).transpose(1, 0, 2).reshape(P, -1))

    lru_w = np.zeros((P, CT, 2, 2, P), np.float32)
    for k, name in enumerate(("lru_wa", "lru_wx")):
        for d in range(2):
            for b in range(HY // LRU_BLOCK):
                o = (b % 2) * LRU_BLOCK
                lru_w[o:o + LRU_BLOCK, b // 2, d, k, o:o + LRU_BLOCK] = a[name][0, d, b]

    filt_in = np.zeros((FILTER_HIDDEN, 384), np.float32)
    filt_in[:33, 0:T] = z
    filt_in[:33, 256:320] = a["hy_w1"][0]
    filt_in[:, 320:384] = a["hy_w2"][0]

    down = a["exp_w_down"][0].reshape(EXPERTS, 4, P, 4, 512).transpose(0, 3, 2, 1, 4).reshape(EXPERTS, 4, P, CHUNK)
    ups = [a[n][0].reshape(EXPERTS, 4, 4, P, 512).transpose(0, 1, 3, 2, 4).reshape(EXPERTS, 4, P, CHUNK)
           for n in ("exp_w_gate", "exp_w_up")]
    w_exp = np.stack([ups[0], ups[1], down])
    w_exp = w_exp.reshape(3, PAIRS, 2, 4, P, CHUNK).transpose(1, 0, 3, 2, 4, 5).reshape(-1, P, CHUNK)

    def tiles(x):
        return x.reshape(T, KT, P).transpose(2, 1, 0).reshape(P, -1)

    arrays = {
        "w_ada": _panels(a["w_ada"][0]),
        "w_in": _panels(a["w_in"][0]).reshape(20, 4, P, CHUNK)[IN_ORDER].reshape(-1, P, CHUNK),
        "w_br": _panels(np.concatenate([a["w_br_attn"][0], a["w_br_hy"][0], a["w_br_lru"][0]])),
        "w_out": _panels(a["w_out"][0]),
        "w_exp": w_exp,
        "x_t": tiles(a["x"][0]),
        "ctx_t": tiles(a["ctx"][0]),
        "params": par,
        "consts": consts,
        "lru_w": lru_w.reshape(P, -1),
        "windows": windows,
        "filt_in": filt_in,
        "filt_w": a["hy_w3"][0],
    }
    arrays = {k: np.ascontiguousarray(v) for k, v in arrays.items()}
    nc = bacc.Bacc("TRN2", target_bir_lowering=False, num_devices=1, dynamic_dma_scratch_size=1024)
    args = [nc.dram_tensor(n, v.shape, mybir.dt.from_np(v.dtype), kind="ExternalInput").ap() for n, v in arrays.items()]
    out = nc.dram_tensor("out_t", (P, KT * T), F32, kind="ExternalOutput").ap()
    build(nc, *args, out)
    r = run_bass_kernel_spmd(nc, [arrays], core_ids=[0])
    got = np.asarray(r.results[0]["out_t"])
    return got.reshape(P, KT, T).transpose(2, 1, 0).reshape(1, T, D)
```

```python
from contextlib import ExitStack, contextmanager

import numpy as np

import concourse.bass as bass
from concourse import mybir

F32 = mybir.dt.float32
F32R = mybir.dt.float32r
I32 = mybir.dt.int32
ALU = mybir.AluOpType
ACT = mybir.ActivationFunctionType
AX = mybir.AxisListType

P = 128
D = 2048
KT = D // P
T = 256
EPS = 1e-6
HEADS, KV_HEADS, HD = 8, 2, 128
GRID_W = 64
WINDOW = 128
HY = D // 4
CT = HY // P
LRU_BLOCK = 64
BANDS = 16
FILTER_HIDDEN = 64
EXPERTS, GROUPS = 16, 4
SLOTS = 64
MAX_ROUNDS = T // SLOTS
RING = 8
CHUNK = 4 * 512
MOE_RING = 12
ADA_PANELS = 6 * D // 512
ADA_FIRST = 8
PAIRS = EXPERTS // 2
PAIR_CHUNKS = 24
START = 1
TWO_PI = 2.0 * np.pi
ROUND_MAGIC = 1.5 * 2.0 ** 23
NEG = -1.0e30
LRU_SLOTS = (0, 2, 5, 7)
ROTATE_SLOTS = {9: (0,), 10: (1, 2), 11: (3, 4)}
VALUE_SLOT = 12
SCORE_SLOT = 12
Y_SLOT = 15
HYENA_SLOTS = (0, 1, 3, 4, 5, 7)
TWO_PI_PARTS = (6.28125, 0.0019350051879882812, 3.0199159795074593e-07)

_PARAM_WIDTHS = [
    ("cond", 2 * KT), ("b_ada", 12 * KT), ("g_mix", 2 * KT), ("g_ffn", KT), ("final_g", KT), ("sink", HEADS),
    ("hy_w", 36), ("hy_b", 12), ("skip", 8), ("lru_w", 16), ("lru_b", 4), ("lru_ba", 8), ("lru_bx", 8),
    ("lam", 8), ("freq", 1), ("fb1", 1), ("fb2", 1), ("router_b", EXPERTS), ("router_w", KT * EXPERTS),
]
_CONST_WIDTHS = [
    ("ident", P), ("ones", P), ("before", P), ("rot", P), ("iota", SLOTS), ("eps", 1),
    ("down16", EXPERTS), ("down4", GROUPS), ("dft", 2 * 512), ("idft", 4 * T), ("rope", 2 * T), ("mask", 2 * 512),
]


def columns(widths):
    at, out = 0, {}
    for name, w in widths:
        out[name] = (at, at + w)
        at += w
    return out, at


PARAM_AT, PARAM_N = columns(_PARAM_WIDTHS)
CONST_AT, CONST_N = columns(_CONST_WIDTHS)


class Steps:

    def __init__(self, eng, sem):
        self.eng, self.sem, self.base, self.n = eng, sem, 0, 0

    def inc(self, ins):
        ins.then_inc(self.sem, 1)
        self.n += 1

    def wait(self):
        self.eng.wait_ge(self.sem, self.base + self.n)

    def done(self, ins):
        self.inc(ins)
        self.wait()

    @contextmanager
    def loop(self, i, count, per):
        start = self.base + self.n
        self.base, self.n = start + i * per, 0
        yield
        assert self.n == per, self.n
        self.base, self.n = start + count * per, 0


def build(nc, w_ada, w_in, w_br, w_out, w_exp, x_t, ctx_t, params, consts, lru_w, windows, filt_in, filt_w, out):
    with ExitStack() as ctx:
        def sb(name, shape, dt=F32):
            return ctx.enter_context(nc.sbuf_tensor(name, shape, dt))

        def sem(name):
            return ctx.enter_context(nc.semaphore(name))

        SPLIT_BUFFERS = (("ring", [P, RING, 4, 512]), ("norm_x", [P, 2, KT, T]), ("proj", [P, 24, T]),
                         ("spec", [P, 4, 2, HY]), ("arena", [P, 6144]), ("kvx", [P, 8, 2, T]), ("lru_m", [P, 16, P]))
        with ExitStack() as views:
            ring_r, norm_r, proj_r, spec_r, arena_r, kvx_r, lru_m_r = (
                views.enter_context(nc.sbuf_tensor(name + "_r", shape, F32R)) for name, shape in SPLIT_BUFFERS)
        ring, norm_x, proj, spec, arena, kvx, lru_m = (sb(name, shape) for name, shape in SPLIT_BUFFERS)
        par = sb("par", [P, PARAM_N])
        con = sb("con", [P, CONST_N])
        mod = sb("mod", [P, 6 * KT, 2])
        modA = sb("modA", [P, KT, 2])
        silu_c = sb("silu_c", [P, KT, 32])
        arow = sb("arow", [P, 512])
        small = sb("small", [P, 256])
        rounds_i = sb("rounds_i", [1, 1], I32)
        PS = ctx.enter_context(nc.psum_tensor("ps", [P, 8, 512], F32))

        def par_(name, a=0, b=None):
            lo, hi = PARAM_AT[name]
            return par[:, lo + a:hi if b is None else lo + b]

        def con_(name, a=0, b=None):
            lo, hi = CONST_AT[name]
            return con[:, lo + a:hi if b is None else lo + b]

        ident = con_("ident")
        ones = con_("ones")
        dft = con_("dft").rearrange("p (n k) -> p n k", n=2)
        idft = con_("idft").rearrange("p (k t) -> p k t", k=4)
        rope = con_("rope").rearrange("p (a t) -> p a t", a=2)
        mask = con_("mask").rearrange("p (a t) -> p a t", a=2)

        ada_sum = small[:, 212:220]
        hc = norm_x[:, 0]
        hl = norm_x[:, 1]
        kv_flat = kvx[:, :, :, :].rearrange("p a b t -> p (a b t)")
        pr_flat = proj[:, :, :].rearrange("p a t -> p (a t)")
        fw3 = kv_flat[:, 0:2048]
        win = kv_flat[:, 2048:4096].rearrange("p (d n c) -> p d n c", d=2, n=2)
        taps = pr_flat[:, 0:2048].rearrange("p (n d c) -> p n d c", n=2, d=2)
        tapsum = pr_flat[:, 2048:4096].rearrange("p (n d c) -> p n d c", n=2, d=2)
        fin = pr_flat[:, 4096:4096 + 384]
        fa = pr_flat[:, 4480:4736]
        fk = pr_flat[:, 4736:4992]
        fh = pr_flat[:, 4992:5248]
        sq = arena[:, 0:1024].rearrange("p (b t) -> p b t", b=2)
        rbc = arena[:, 1024:1536]
        tsq = arena[:, 1536:3584].rearrange("p (n d c) -> p n d c", n=2, d=2)
        tsum = arena[:, 3584:4608].rearrange("p (o c) -> p o c", o=2)
        xc = arena[:, 0:2048].rearrange("p (c t) -> p c t", c=4)
        lA = [arena[:, 2048 + 512 * d:2560 + 512 * d] for d in range(2)]
        lB = [arena[:, 3072 + 512 * d:3584 + 512 * d] for d in range(2)]
        lT = [arena[:, 4096 + 512 * d:4608 + 512 * d] for d in range(2)]
        lU = arena[:, 5120:5632]
        rtmp = arena[:, 5632:6144]
        hv = arena[:, 0:1024].rearrange("p (c t) -> p c t", c=4)
        ztok = arena[:, 1024:2048].rearrange("p (n c) -> p n c", n=2)
        ysp = arena[:, 2048:4096].rearrange("p (k c) -> p k c", k=4)
        ht = [arena[:, 4096 + 512 * i:4608 + 512 * i] for i in range(2)]
        s_sb = [arena[:, 2048 + 512 * i:2560 + 512 * i] for i in range(2)]
        p_t = [arena[:, 3072 + 1024 * i:4096 + 1024 * i].rearrange("p (k q) -> p k q", k=4) for i in range(2)]
        v_tok = arena[:, 5120:6144].rearrange("p (k c) -> p k c", k=4)
        spec_flat = spec[:, :, :, :].rearrange("p a b c -> p (a b c)")
        m_t = spec_flat.rearrange("p (k t) -> p k t", k=KT)
        gates = [kv_flat[:, 1024 * j:1024 * j + 1024] for j in range(3)]
        gtmp = kv_flat[:, 3072:4096]
        w_hi = [arena_r[:, 1024 + 2048 * i:3072 + 2048 * i].rearrange("p (a c) -> p a c", a=4) for i in range(2)]
        kv_r = kvx_r[:, :, :, :].rearrange("p a b t -> p (a b t)")
        early_hi = [[proj_r[:, 8 + 8 * i:16 + 8 * i, :].rearrange("p a t -> p (a t)").rearrange("p (a c) -> p a c", a=4) for i in range(2)],
                    [kv_r[:, 2048:4096].rearrange("p (a c) -> p a c", a=4),
                     lru_m_r[:, :, :].rearrange("p u m -> p (u m)").rearrange("p (a c) -> p a c", a=4)]]
        hl_hi, hl_lo = norm_r[:, 0], norm_r[:, 1]
        both_hi = [b.rearrange("p (k s t) -> p k s t", k=8, s=2) for b in (
            proj_r[:, 0:16, :].rearrange("p a t -> p (a t)"), arena_r[:, 0:4096])]
        wide_hi = [proj_r[:, 16:24, :].rearrange("p a t -> p (a t)").rearrange("p (a c) -> p a c", a=4),
                   arena_r[:, 4096:6144].rearrange("p (a c) -> p a c", a=4)]
        mix_hi, mix_lo = proj_r[:, 12:24, :], proj_r[:, 0:12, :]
        hv_hi = arena_r[:, 5120:6144].rearrange("p (c t) -> p c t", c=4)
        hv_lo = arena_r[:, 0:1024].rearrange("p (c t) -> p c t", c=4)
        m_hi = norm_r[:, 1]
        m_lo = spec_r[:, :, :, :].rearrange("p a b c -> p (a b c)").rearrange("p (k t) -> p k t", k=KT)
        sqn = arena[:, 5120:5376]
        rbn = arena[:, 5632:5888]
        sqsum = arena[:, 5888:6144]
        rlog = arena[0:EXPERTS, 5120:5376]
        x_res = kvx[:, :, :, :].rearrange("p a b t -> p (a b) t")
        moe_ring = [ring[:, s] for s in range(RING)]
        hc_flat = hc.rearrange("p k t -> p (k t)")
        moe_ring += [hc_flat[:, 2048 * i:2048 * i + 2048].rearrange("p (a c) -> p a c", a=4) for i in range(2)]
        moe_ring += [con[:, CONST_AT["dft"][0]:CONST_AT["idft"][1]].rearrange("p (a c) -> p a c", a=4),
                     lru_m[:, :, :].rearrange("p u m -> p (u m)").rearrange("p (a c) -> p a c", a=4)]
        fl = hl
        xg = [m_t, hl]
        fl_tok = pr_flat[:, 0:4096].rearrange("p (n c) -> p n c", n=2)
        yg = pr_flat[:, 4096:6144]
        squares = hl
        sg = arena[:, 0:512]
        act_sb = arena[:, 512:1024]
        act_t = arena[:, 1024:1536].rearrange("p (k s) -> p k s", k=4)
        cw_t = arena[:, 1536:1792]
        disp = arena[:, 1792:2304].rearrange("p (n s) -> p n s", n=2)
        comb = arena[:, 2304:2816].rearrange("p (n s) -> p n s", n=2)
        rt = arena[:, 3072:3840]
        rank = arena[:, 3840:3872]
        weight = arena[:, 3872:3904]

        ring_in = [sem(f"ring_in{s}") for s in range(RING)]
        ring_out = sem("ring_out")
        moe_in = [sem(f"moe_in{s}") for s in range(MOE_RING)]
        moe_out = sem("moe_out")
        names = """in_par in_con in_late in_x in_ctx in_filt in_fw3 in_win in_lru in_res
            silu_zero silu_ready ada_copied ada_turned ada_summed ada_added
            sq_ready norm_mm norm_root norm_ready h_ready
            arg_mm arg_ready sin_ready tap_mm tapsum_ready spec_mm spec_copied tnorm_mm tnorm_root
            kv_dve kv_act nar_dve nar_act
            lam_exp lam_ready lru_in lru_mm lru_gate lru_tanh lru_exp lru_var lru_root gelu_ready
            rot_mm rot_used vt_mm vt_copied
            sc_mm sc_read sc_bias p_exp p_ready pt_mm pt_copied pv_mm pv_copied
            lru_done hy_in hy_tmm hy_tcopied hy_fmm hy_ready hy_imm mix_done
            early_split_hi early_split_lo both_high both_low latent_hi
            split_hi split_lo operand_hi operand_lo gate_sig br_used summed merged out_used
            sq2_ready norm2_mm norm2_root fl_scaled fl_ready ft_mm ft_copied
            router_mm router_sb router_turned router_exp router_arg pick_ready rank_mm route_ready
            disp_ready comb_ready acc_mm acc_done silu_done act_ready at_mm at_copied dn_copied ct_mm ct_copied
            y_ready sq3_ready sq4_ready norm3_mm norm3_root out_ready out_done dve_main dve_moe dve_end""".split()
        S = {n: sem(n) for n in names}
        (in_par, in_con, in_late, in_x, in_ctx, in_filt, in_fw3, in_win, in_lru, in_res,
         silu_zero, silu_ready, ada_copied, ada_turned, ada_summed, ada_added,
         sq_ready, norm_mm, norm_root, norm_ready, h_ready,
         arg_mm, arg_ready, sin_ready, tap_mm, tapsum_ready, spec_mm, spec_copied, tnorm_mm, tnorm_root,
         kv_dve, kv_act, nar_dve, nar_act,
         lam_exp, lam_ready, lru_in, lru_mm, lru_gate, lru_tanh, lru_exp, lru_var, lru_root, gelu_ready,
         rot_mm, rot_used, vt_mm, vt_copied,
         sc_mm, sc_read, sc_bias, p_exp, p_ready, pt_mm, pt_copied, pv_mm, pv_copied,
         lru_done, hy_in, hy_tmm, hy_tcopied, hy_fmm, hy_ready, hy_imm, mix_done,
         early_split_hi, early_split_lo, both_high, both_low, latent_hi,
         split_hi, split_lo, operand_hi, operand_lo, gate_sig, br_used, summed, merged, out_used,
         sq2_ready, norm2_mm, norm2_root, fl_scaled, fl_ready, ft_mm, ft_copied,
         router_mm, router_sb, router_turned, router_exp, router_arg, pick_ready, rank_mm, route_ready,
         disp_ready, comb_ready, acc_mm, acc_done, silu_done, act_ready, at_mm, at_copied, dn_copied, ct_mm, ct_copied,
         y_ready, sq3_ready, sq4_ready, norm3_mm, norm3_root, out_ready, out_done, dve_main, dve_moe, dve_end) = S.values()

        T_WIDE = ADA_FIRST * 4 // RING
        T_NAR = T_WIDE + 2
        T_MERGE = T_NAR + 6
        T_OUT = T_MERGE + 4 * 3
        A_NAR = ADA_FIRST + 2
        A_MERGE = A_NAR + 6

        def moe_slot(c):
            return (c + RING) % MOE_RING

        def used(turn, slots):
            return turn * RING + slots

        def split_waits(i):
            at = i if i < 12 else i + 4
            free = {0: -5, 1: -4, 12: 11, 13: 12}.get(i, at - 1)
            return at // RING, at % RING, free

        block = ctx.enter_context(nc.Block())

        @block.sync
        def _(sp):
            def load(turn, slot, src, first=False):
                if not first:
                    sp.wait_ge(ring_out, used(turn, slot + 1 - RING))
                sp.dma_start(ring[:, slot].rearrange("p a n -> p (a n)"), src).then_inc(ring_in[slot], 16)

            for s in range(RING):
                load(0, s, w_ada[s], first=True)
            with sp.Fori(1, T_WIDE) as i:
                for s in range(RING):
                    load(i, s, w_ada[i * RING + s])
            with sp.Fori(0, 8) as i:
                for s in range(4):
                    load(i + T_WIDE, s, w_in[i * 4 + s])
                for s in range(4):
                    load(i + T_WIDE, 4 + s, w_ada[i * 4 + (4 * ADA_FIRST + s)])
            with sp.Fori(0, 4) as n:
                for j in range(3):
                    for q in range(4):
                        c = 4 * j + q
                        load(n * 3 + (T_MERGE + c // RING), c % RING, w_in[n * 4 + (32 + 16 * j + q)])
                for q in range(4):
                    load(n * 3 + (T_MERGE + 1), 4 + q, w_ada[n * 8 + (4 * A_MERGE + q)])
                for q in range(4):
                    load(n * 3 + (T_MERGE + 2), q, w_br[n * 4 + q])
                for q in range(4):
                    load(n * 3 + (T_MERGE + 2), 4 + q, w_ada[n * 8 + (4 * A_MERGE + 4 + q)])
            def load_expert(it, c, src):
                s = moe_slot(c)
                sp.dma_start(moe_ring[s].rearrange("p a n -> p (a n)"), src).then_inc(moe_in[s], 16)

            sp.wait_ge(ring_out, used(T_OUT - 2, 4))
            for s in range(RING):
                load(T_OUT, s, w_out[s])
            for c in range(4):
                load_expert(0, c, w_exp[c])
            for s in range(RING):
                load(T_OUT + 1, s, w_out[RING + s])

            def group(it, g, first=0):
                for c in range(first, 2 * PAIR_CHUNKS):
                    sp.wait_ge(moe_out, it * (2 * PAIR_CHUNKS) + (c - MOE_RING + 1))
                    load_expert(it, c, w_exp[g * (2 * PAIR_CHUNKS) + c])

            for c in range(4, MOE_RING):
                sp.wait_ge(ring_out, used(T_OUT + 1, c - 3))
                load_expert(0, c, w_exp[c])
            group(0, 0, MOE_RING)
            with sp.Fori(1, 4) as g:
                group(g, g)
            sp.wait_ge(route_ready, 1)
            nr = sp.value_load(rounds_i[0:1, 0:1], min_val=1, max_val=MAX_ROUNDS)
            with sp.If(nr > 1):
                with sp.Fori(1, nr) as r:
                    with sp.Fori(0, 4) as g:
                        group(r * 4 + g, g)
            for q in range(4):
                sp.wait_ge(out_ready, q + 1)
                sp.dma_start(out[:, q * 4 * T:(q + 1) * 4 * T],
                             x_res[:, 4 * q:4 * q + 4, :].rearrange("p k t -> p (k t)")).then_inc(out_done, 16)
            sp.wait_ge(out_done, 64)

        @block.tensor
        def _(pe):
            for begun in (ada_turned, acc_mm, at_mm):
                pe.sem_inc(begun, START)
            def mm(o, l, r, start=True, stop=True, **kw):
                return pe.matmul(o, l, r, start=start, stop=stop, **kw)

            def chunk(turn, slot):
                pe.wait_ge(ring_in[slot], (turn + 1) * 16)

            def ada_panel(a, turn, slot0):
                pe.wait_ge(ada_copied, START + a)
                for q in range(4):
                    chunk(turn, slot0 + q)
                    for k in range(4):
                        last = mm(PS[32 * k:32 * k + 32, 6, :], silu_c[:, 4 * q + k, :], ring[:, slot0 + q, k, :],
                                  start=q == 0, stop=q == 3, tile_position=(0, 32 * k))
                    last.then_inc(ring_out, 1)

            def ada_turn(a):
                pe.wait_ge(ada_copied, START + a + 1)
                pe.wait_ge(ada_added, START + a)
                for c in range(4):
                    last = pe.transpose(PS[:, 7, c * P:(c + 1) * P], arow[:, c * P:(c + 1) * P], ident)
                last.then_inc(ada_turned, 1)

            def panel(bank, slot0, first, hi, lo, tiles=KT, ready=None, early=False, weave=None):
                for q in range(tiles // 4):
                    if not early:
                        pe.wait_ge(split_lo, first + (q + 1))
                    if ready:
                        ready(q)
                    high = (early[(slot0 + q) % 2] if early else w_hi[(slot0 + q) % 2])
                    low = ring_r[:, slot0 + q]
                    for k in range(4):
                        if early and k % 2 == 0:
                            pe.wait_ge(early_split_lo, 2 * (first + q) + k // 2 + 1)
                        kt = 4 * q + k
                        for c in range(4):
                            o = PS[:, bank + c // 2, (c % 2) * T:(c % 2 + 1) * T]
                            wh = high[:, k, c * P:(c + 1) * P]
                            wl = low[:, k, c * P:(c + 1) * P]
                            mm(o, wl, hi(kt), start=kt == 0 and c % 2 == 0, stop=False, skip_group_check=True)
                            mm(o, wh, lo(kt), start=False, stop=False, skip_group_check=True)
                            last = mm(o, wh, hi(kt), start=False, stop=kt == tiles - 1, skip_group_check=True)
                    last.then_inc(ring_out, 1)
                    if weave:
                        weave(q)

            latent = (lambda kt: hl_hi[:, kt, :], lambda kt: hl_lo[:, kt, :])

            def filter_input(i):
                if i == 0:
                    pe.wait_ge(in_filt, 16)
                    mm(PS[0:FILTER_HIDDEN, 4, 0:T], fin[0:33, 256:320], fin[0:33, 0:256]).then_inc(arg_mm, 1)
                else:
                    pe.wait_ge(sin_ready, 1)
                    mm(PS[0:FILTER_HIDDEN, 3, 0:T], fin[0:64, 320:384], fh[0:64, :]).then_inc(arg_mm, 1)

            def mean_squares():
                for kt in range(KT):
                    pe.wait_ge(sq_ready, kt + 1)
                    mm(PS[:, 5, :], ones, sq[:, kt % 2], start=kt == 0, stop=kt == KT - 1).then_inc(norm_mm, 1)

            def filter_taps(o):
                if o == 0:
                    pe.wait_ge(sin_ready, 2)
                    pe.wait_ge(in_fw3, 16)
                for u in range(4):
                    nt, d = u // 2, u % 2
                    if o:
                        pe.wait_ge(spec_copied, u + 1)
                    mm(PS[:, u, :], fh[0:64, nt * P:(nt + 1) * P],
                       fw3[0:64, (2 * o + d) * 512:(2 * o + d + 1) * 512]).then_inc(tap_mm, 1)

            def filter_spectrum(o):
                pe.wait_ge(tapsum_ready, o + 1)
                for u in range(4):
                    cs, kk = u // 2, u % 2
                    for nt in range(2):
                        last = mm(PS[:, u, :], dft[:, nt, cs * T + kk * P:cs * T + (kk + 1) * P],
                                  tapsum[:, nt, cs, :], start=nt == 0, stop=nt == 1)
                    last.then_inc(spec_mm, 1)

            def filter_norm():
                for o in range(2):
                    for c in range(CT):
                        last = mm(PS[:, 4, 4 * o + c:4 * o + c + 1], tsum[:, o, c * P:(c + 1) * P], ones[:, 0:1])
                last.then_inc(tnorm_mm, 1)

            pe.wait_ge(silu_ready, 1)
            for a in range(ADA_FIRST):
                ada_panel(a, a // 2, 4 * (a % 2))
                if a == 0:
                    pe.wait_ge(in_con, 16)
                ada_turn(a)
                if a == 0:
                    mean_squares()
                if a in (1, 2):
                    filter_input(a - 1)
                if a in (3, 5):
                    filter_taps((a - 3) // 2)
                if a in (4, 6):
                    filter_spectrum((a - 4) // 2)
                if a == 6:
                    filter_norm()

            pe.wait_ge(spec_copied, 8)
            pe.wait_ge(tnorm_root, 1)
            for i in range(2):
                if i:
                    pe.wait_ge(kv_dve, 2)
                    pe.wait_ge(kv_act, 2)
                for q in range(4):
                    for k in range(4):
                        kt = 4 * q + k
                        if k % 2 == 0:
                            pe.wait_ge(early_split_lo, 2 * (4 * i + q) + k // 2 + 1)
                        if i == 0:
                            pe.wait_ge(both_low, kt + 1)
                        high, low = both_hi[kt // 8][:, kt % 8], norm_r[:, :, kt, :]
                        for c in range(4):
                            wh, wl = wide_hi[q % 2][:, k, c * P:(c + 1) * P], ring_r[:, q, k, c * P:(c + 1) * P]
                            mm(PS[:, c, :], wl, high, start=kt == 0, stop=False)
                            mm(PS[:, c, :], wh, low, start=False, stop=False)
                            last = mm(PS[:, c, :], wh, high, start=False, stop=kt == KT - 1)
                    last.then_inc(ring_out, 1)
                ada_panel(ADA_FIRST + i, T_WIDE + i, 4)
                ada_turn(ADA_FIRST + i)
            def lru_gates(c):
                if c == 0:
                    pe.wait_ge(in_lru, 16)
                pe.wait_ge(lru_in, c + 1)
                if c:
                    pe.wait_ge(lru_gate, 4 * c)
                for u in range(4):
                    mm(PS[:, 2 + u, :], lru_m[:, 4 * c + u, :], xc[:, c, :]).then_inc(lru_mm, 1)

            def rotate(u):
                pe.wait_ge(lru_gate, 16)
                if u >= 2:
                    pe.wait_ge(rot_used, u - 1)
                src = kvx[:, 0:2, 1, :] if u == 0 else proj[:, 2 * u - 2:2 * u, :]
                mm(PS[:, 4 + u % 2, :], con_("rot"), src).then_inc(rot_mm, 1)

            def turn_values():
                pe.wait_ge(rot_used, 5)
                for kk in range(4):
                    for h in range(KV_HEADS):
                        last = pe.transpose(PS[:, 4 + kk // 2, (kk % 2) * T + h * P:(kk % 2) * T + (h + 1) * P],
                                            kvx[:, 2 + h, kk // 2, (kk % 2) * P:(kk % 2 + 1) * P], ident)
                last.then_inc(vt_mm, 1)

            def scores(u):
                h, qt = u // 2, u % 2
                if u >= 2:
                    pe.wait_ge(sc_read, u - 1)
                pe.wait_ge(rot_used, 5)
                mm(PS[:, 2 + u % 2, :], proj[:, h, qt * P:(qt + 1) * P], kvx[:, h // 4, :, :]).then_inc(sc_mm, 1)

            def turn_probs(u):
                pe.wait_ge(p_ready, u + 1)
                if u:
                    pe.wait_ge(pt_copied, u)
                else:
                    pe.wait_ge(vt_copied, 1)
                for kk in range(4):
                    last = pe.transpose(PS[:, 4, kk * P:(kk + 1) * P], s_sb[u % 2][:, kk * P:(kk + 1) * P], ident)
                last.then_inc(pt_mm, 1)

            def values(h):
                pe.wait_ge(pt_copied, 2 * h + 2)
                if h:
                    pe.wait_ge(pv_copied, h)
                for kk in range(4):
                    last = mm(PS[:, 5, 0:T], v_tok[:, kk, (h // 4) * P:(h // 4 + 1) * P],
                              p_t[h % 2][:, kk, :], start=kk == 0, stop=kk == 3)
                last.then_inc(pv_mm, 1)

            def weave_mixers(slot):
                if slot in LRU_SLOTS:
                    lru_gates(LRU_SLOTS.index(slot))
                for u in ROTATE_SLOTS.get(slot, ()):
                    rotate(u)
                if slot == VALUE_SLOT:
                    turn_values()
                u = slot - SCORE_SLOT
                if 0 <= u < 16:
                    scores(u)
                if 1 <= u <= 16:
                    turn_probs(u - 1)
                if u >= 3 and u % 2 == 1 and u <= 17:
                    values((u - 3) // 2)

            pe.wait_ge(in_late, 16)
            pe.wait_ge(kv_dve, 4)
            pe.wait_ge(kv_act, 4)
            for i in range(6):
                pe.wait_ge(nar_dve, START + i)
                pe.wait_ge(nar_act, START + i)
                panel(0, 0, 8 + 4 * i, *latent, early=early_hi[i // 2 and 1], ready=lambda q: pe.wait_ge(latent_hi, q + 1),
                      weave=lambda q: weave_mixers(5 * i + q))
                ada_panel(A_NAR + i, T_NAR + i, 4)
                ada_turn(A_NAR + i)
                weave_mixers(5 * i + 4)

            def hyena_turn(o):
                pe.wait_ge(hy_in, o + 1)
                for nt in range(2):
                    for c in range(CT):
                        last = pe.transpose(PS[:, 4 + nt, c * P:(c + 1) * P], hv[:, c, nt * P:(nt + 1) * P], ident)
                    last.then_inc(hy_tmm, 1)

            def hyena_forth(o):
                pe.wait_ge(hy_tcopied, 2 * o + 2)
                for u in range(4):
                    kk, cs = u // 2, u % 2
                    for nt in range(2):
                        last = mm(PS[:, 2 + u, :], dft[:, nt, cs * T + kk * P:cs * T + (kk + 1) * P], ztok[:, nt, :],
                                  start=nt == 0, stop=nt == 1)
                    last.then_inc(hy_fmm, 1)

            def hyena_back(o):
                pe.wait_ge(hy_ready, o + 1)
                for c in range(CT):
                    for kk in range(4):
                        last = mm(PS[:, 2 + c // 2, (c % 2) * T:(c % 2 + 1) * T], ysp[:, kk, c * P:(c + 1) * P],
                                  idft[:, kk, :], start=kk == 0, stop=kk == 3)
                    last.then_inc(hy_imm, 1)

            def weave_hyena(slot):
                if slot in HYENA_SLOTS:
                    k = HYENA_SLOTS.index(slot)
                    (hyena_turn, hyena_forth, hyena_back)[k % 3](k // 3)

            BRANCHES = ((0, 8), (2, 4), (3, 4))
            inputs_lo = (lambda k: mix_lo[:, k, :], lambda k: hv_lo[:, k, :], lambda k: mix_lo[:, 8 + k, :])
            inputs_hi = (lambda k: mix_hi[:, k, :], lambda k: hv_hi[:, k, :], lambda k: mix_hi[:, 8 + k, :])

            def merge_first():
                for j in range(3):
                    if j:
                        pe.wait_ge(gate_sig, j)
                    panel(0, 4 * (j % 2), 32 + 4 * j, *latent, early=early_hi[1], weave=lambda q: weave_hyena(4 * j + q))
                ada_panel(A_MERGE, T_MERGE + 1, 4)
                ada_turn(A_MERGE)
                pe.wait_ge(gate_sig, 3)
                pe.wait_ge(operand_lo, 2)
                for j, (q0, tiles) in enumerate(BRANCHES):
                    panel(2 * j, q0, q0, inputs_hi[j], inputs_lo[j], tiles)
                ada_panel(A_MERGE + 1, T_MERGE + 2, 4)
                ada_turn(A_MERGE + 1)

            def merge_part(n):
                first = n * 16 - 12
                for j in range(3):
                    pe.wait_ge(br_used, n * 3 + (START - 2 + j))
                    panel(2 * j, 4 * (j % 2), first + 4 * j, *latent)
                ada_panel(n * 2 + A_MERGE, n * 3 + (T_MERGE + 1), 4)
                ada_turn(n * 2 + A_MERGE)
                for j, (q0, tiles) in enumerate(BRANCHES):
                    pe.wait_ge(gate_sig, n * 3 + (j + 1))
                    panel(2 * j, q0, first + (12 + q0), inputs_hi[j], inputs_lo[j], tiles)
                ada_panel(n * 2 + (A_MERGE + 1), n * 3 + (T_MERGE + 2), 4)
                ada_turn(n * 2 + (A_MERGE + 1))

            pe.wait_ge(nar_dve, START + 6)
            pe.wait_ge(nar_act, START + 6)
            pe.wait_ge(lru_done, 1)
            pe.wait_ge(sc_read, 16)
            pe.wait_ge(pt_copied, 16)
            pe.wait_ge(pv_copied, 8)
            merge_first()
            with pe.Fori(1, 4) as n:
                merge_part(n)
            pe.wait_ge(br_used, START + 12)
            with pe.Fori(0, 2) as i:
                for h in range(2):
                    pe.wait_ge(out_used, i * (h + 1) + START)
                    panel(2 * h, 4 * h, i * 8 + (52 + 4 * h), lambda kt: m_hi[:, kt, :], lambda kt: m_lo[:, kt, :],
                                ready=lambda q: pe.wait_ge(operand_lo, 3 + q))
            pe.wait_ge(sq2_ready, 1)
            mm(PS[:, 5, 0:T], ones, sqsum).then_inc(norm2_mm, 1)

            def turn_tokens(w):
                q, tt = w // 2, w % 2
                if w >= 4:
                    pe.wait_ge(ft_copied, w - 3)
                for k in range(4):
                    last = pe.transpose(PS[:, w % 4, k * P:(k + 1) * P], fl[:, 4 * q + k, tt * P:(tt + 1) * P], ident)
                last.then_inc(ft_mm, 1)

            for kt in range(KT):
                pe.wait_ge(fl_ready, kt + 1)
                last = mm(PS[0:EXPERTS, 4, 0:T], par_("router_w", kt * EXPERTS, (kt + 1) * EXPERTS), fl[:, kt, :],
                          start=kt == 0, stop=kt == KT - 1)
            last.then_inc(router_mm, 1)
            turn_tokens(0)
            turn_tokens(1)
            pe.wait_ge(router_sb, 1)
            for tt in range(2):
                last = pe.transpose(PS[:, 5, 64 + tt * EXPERTS:64 + (tt + 1) * EXPERTS], rlog[:, tt * P:(tt + 1) * P], ident[0:EXPERTS, 0:EXPERTS])
            last.then_inc(router_turned, 1)
            for w in range(2, 8):
                turn_tokens(w)
            pe.wait_ge(pick_ready, 1)
            chosen = [rt[:, 0:16], rt[:, 16:32]]
            mm(PS[:, 5, 0:16], con_("before"), chosen[0])
            mm(PS[:, 5, 16:32], ones, chosen[0], start=True, stop=False)
            mm(PS[:, 5, 16:32], con_("before"), chosen[1], start=False, stop=True)
            mm(PS[:, 5, 32:48], ones, chosen[0], start=True, stop=False)
            mm(PS[:, 5, 32:48], ones, chosen[1], start=False, stop=True).then_inc(rank_mm, 1)
            pe.wait_ge(ft_copied, 8)
            pe.wait_ge(route_ready, 1)
            nr = pe.value_load(rounds_i[0:1, 0:1], min_val=1, max_val=MAX_ROUNDS)

            def gather(it, turn, v):
                pe.wait_ge(disp_ready, it + 1)
                if turn is not None:
                    pe.wait_ge(acc_done, turn + (START - 1))
                for f in range(2):
                    for tt in range(2):
                        last = mm(PS[:, 6 + v % 2, f * T:(f + 1) * T], fl_tok[:, tt, (2 * v + f) * P:(2 * v + f + 1) * P],
                                  disp[:, tt, :], start=tt == 0, stop=tt == 1)
                last.then_inc(acc_mm, 1)

            for v in range(8):
                gather(0, v if v >= 2 else None, v)
            pe.wait_ge(acc_done, START + 8)

            def group(it, now):
                pe.wait_ge(acc_done, START + it * 24)
                for p in range(2):
                    pair = it * 2 + p
                    c0 = PAIR_CHUNKS * p

                    def expert_chunk(c):
                        s = moe_slot(c)
                        pe.wait_ge(moe_in[s], (it * 4 + (c // MOE_RING + 1)) * 16)
                        return moe_ring[s]

                    for part in range(2):
                        if part == 0:
                            pe.wait_ge(silu_done, START + pair)
                        else:
                            pe.wait_ge(act_ready, START + pair)
                        for q in range(4):
                            w = [expert_chunk(c0 + 8 * part + 2 * q + e) for e in range(2)]
                            for k in range(4):
                                kt = 4 * q + k
                                for e in range(2):
                                    last = mm(PS[64 * e:64 * e + 64, part, :], xg[now][:, kt, (2 * p + e) * SLOTS:(2 * p + e + 1) * SLOTS],
                                              w[e][:, k, :], start=kt == 0, stop=kt == KT - 1,
                                              tile_position=(0, 64 * e))
                                    if k == 3:
                                        last.then_inc(moe_out, 1)
                            if q % 2:
                                v = 4 * p + 2 * part + q // 2
                                gather(it + 1, it * 24 + (8 + 12 * p + 2 * part + q // 2), v)
                    pe.wait_ge(comb_ready, it + 1)
                    pe.wait_ge(ct_copied, START + pair)
                    for tt in range(2):
                        last = pe.transpose(PS[:, 3, tt * P:(tt + 1) * P], comb[:, tt, p * P:(p + 1) * P], ident)
                    last.then_inc(ct_mm, 1)
                    pe.wait_ge(act_ready, START + pair + 1)
                    pe.wait_ge(at_copied, START + pair)
                    for k in range(4):
                        last = pe.transpose(PS[:, 2, k * P:(k + 1) * P], act_sb[:, k * P:(k + 1) * P], ident)
                    last.then_inc(at_mm, 1)
                    pe.wait_ge(at_copied, START + pair + 1)
                    for n in range(4):
                        pe.wait_ge(dn_copied, START + pair * 4 + (n - 1 if n >= 2 else 0))
                        w = [expert_chunk(c0 + 16 + 2 * n + e) for e in range(2)]
                        for k in range(4):
                            for e in range(2):
                                last = mm(PS[64 * e:64 * e + 64, 4 + n % 2, :], act_t[:, k, e * SLOTS:(e + 1) * SLOTS],
                                          w[e][:, k, :], start=k == 0, stop=k == 3, tile_position=(0, 64 * e))
                                if k == 3:
                                    last.then_inc(moe_out, 1)
                    pe.wait_ge(dn_copied, START + pair * 4 + 4)
                    pe.wait_ge(ct_copied, START + pair + 1)
                    for v in range(8):
                        pe.wait_ge(acc_done, START + it * 24 + (8 + 12 * p + 4 + v - 1))
                        for f in range(2):
                            last = mm(PS[:, 6 + v % 2, f * T:(f + 1) * T], yg[:, (2 * v + f) * P:(2 * v + f + 1) * P], cw_t)
                        last.then_inc(acc_mm, 1)

            with pe.Fori(0, nr) as r:
                with pe.Fori(0, 2) as h:
                    for now in range(2):
                        group(r * 4 + h * 2 + now, now)
            for kt in range(KT):
                pe.wait_ge((sq3_ready, sq4_ready)[kt % 2], kt // 2 + 1)
                last = mm(PS[:, 5, 0:T], ones, squares[:, kt, :], start=kt == 0, stop=kt == KT - 1)
            last.then_inc(norm3_mm, 1)

        @block.scalar
        def _(act):
            for begun in (ada_copied, nar_act, silu_done, at_copied, dn_copied):
                act.sem_inc(begun, START)
            act.dma_start(par[:, :], params).then_inc(in_par, 16)
            late = CONST_AT["idft"][0]
            act.dma_start(con[:, 0:late], consts[:, 0:late]).then_inc(in_con, 16)
            act.dma_start(hl.rearrange("p k t -> p (k t)"), x_t).then_inc(in_x, 16)
            act.dma_start(hc.rearrange("p k t -> p (k t)"), ctx_t).then_inc(in_ctx, 16)
            act.dma_start(fin[0:64, :], filt_in).then_inc(in_filt, 16)
            act.dma_start(fw3[0:64, :], filt_w).then_inc(in_fw3, 16)
            act.dma_start(win.rearrange("p d n c -> p (d n c)"), windows).then_inc(in_win, 16)
            f = act.activation

            act.wait_ge(in_par, 16)
            act.wait_ge(silu_zero, 1)
            f(silu_c[:, :, 0:2], par_("cond").rearrange("p (k b) -> p k b", b=2), ACT.Silu).then_inc(silu_ready, 1)
            def ada_copy(a, turn, slots):
                act.wait_ge(ring_out, used(turn, slots))
                act.wait_ge(ada_turned, START + a)
                f(arow[:, :], PS[:, 6, :], ACT.Copy).then_inc(ada_copied, 1)

            def filter_sin(i):
                act.wait_ge(arg_ready, i + 1)
                f(fh[0:64, :], fa[0:64, :], ACT.Sin).then_inc(sin_ready, 1)

            for a in range(ADA_FIRST):
                ada_copy(a, a // 2, 4 * (a % 2) + 4)
                if a in (1, 2):
                    filter_sin(a - 1)
                if a == 0:
                    act.wait_ge(in_con, 16)
                    act.wait_ge(norm_mm, KT)
                    f(rbc, PS[:, 5, :], ACT.Sqrt, bias=con_("eps"), scale=1.0 / D).then_inc(norm_root, 1)
                if a in (4, 6):
                    o = (a - 4) // 2
                    for u in range(4):
                        act.wait_ge(spec_mm, 4 * o + u + 1)
                        f(spec[:, u, o, :], PS[:, u, :], ACT.Copy).then_inc(spec_copied, 1)
                if a == 5:
                    act.wait_ge(lam_exp, 1)
                    f(small[:, 24:32], small[:, 16:24], ACT.Exp, scale=-1.0).then_inc(lam_exp, 1)
                if a == 6:
                    act.wait_ge(tnorm_mm, 1)
                    f(small[:, 0:8], PS[:, 4, 0:8], ACT.Sqrt, bias=con_("eps")).then_inc(tnorm_root, 1)
            act.dma_start(lru_m[:, :, :].rearrange("p u m -> p (u m)"), lru_w).then_inc(in_lru, 16)
            act.dma_start(con[:, late:], consts[:, late:]).then_inc(in_late, 16)
            def early_split(n):
                if n < 24:
                    turn0, buffers, i = T_NAR + n // 4, early_hi[n >= 8], n % 4
                else:
                    turn0, buffers, i = T_MERGE, early_hi[1], n - 24
                turn, slot, free = split_waits(i)
                act.wait_ge(ring_in[slot], (turn0 + turn + 1) * 16)
                act.wait_ge(ring_out, turn0 * RING + free)
                if n == 8:
                    act.wait_ge(lru_in, CT)
                if n == 9:
                    act.wait_ge(lru_mm, 4 * CT)
                f(buffers[i % 2], ring[:, slot], ACT.Copy).then_inc(early_split_hi, 1)

            def latent_split(q):
                f(hl_hi[:, 4 * q:4 * q + 4, :], both_hi[q // 2][:, 4 * (q % 2):4 * (q % 2) + 4, 1, :], ACT.Copy).then_inc(latent_hi, 1)

            def wide_split(n):
                turn0, i = T_WIDE + n // 4, n % 4
                act.wait_ge(ring_in[i], (turn0 + 1) * 16)
                if n >= 2:
                    act.wait_ge(ring_out, turn0 * RING + split_waits(i)[2])
                f(wide_hi[i % 2], ring[:, i], ACT.Copy).then_inc(early_split_hi, 1)

            def evacuate(i):
                act.wait_ge(ring_out, used(T_WIDE + i, 4))
                for c in (1, 3):
                    f(kvx[:, 4 * i + c, :, :], PS[:, c, :].rearrange("p (s t) -> p s t", s=2), ACT.Copy).then_inc(kv_act, 1)

            wide_split(0)
            for kt in range(KT):
                act.wait_ge(h_ready, kt + 1)
                f(both_hi[kt // 8][:, kt % 8], norm_x[:, :, kt, :], ACT.Copy).then_inc(both_high, 1)
                if kt in (1, 11, 15):
                    wide_split({1: 1, 11: 2, 15: 3}[kt])
            wide_split(4)
            evacuate(0)
            wide_split(5)
            ada_copy(ADA_FIRST, T_WIDE, 8)
            wide_split(6)
            wide_split(7)
            evacuate(1)
            latent_split(0)
            latent_split(1)
            act.wait_ge(latent_hi, 2)
            early_split(0)
            ada_copy(ADA_FIRST + 1, T_WIDE + 1, 8)
            latent_split(2)
            latent_split(3)
            early_split(1)
            def lru(c):
                if c:
                    act.wait_ge(lru_in, CT + c)
                for u in range(4):
                    act.wait_ge(lru_mm, 4 * c + u + 1)
                    d = u // 2
                    to, b = (lA[d], "lru_ba") if u % 2 == 0 else (lB[d], "lru_bx")
                    f(to, PS[:, 2 + u, :], ACT.Sigmoid, bias=par_(b, 4 * d + c, 4 * d + c + 1)).then_inc(lru_gate, 1)
                act.wait_ge(lam_ready, 1)
                act.wait_ge(lru_gate, 4 * c + 4)
                for d in range(2):
                    f(lT[d], lA[d], ACT.Tanh, scale=small[:, 32 + 4 * d + c:33 + 4 * d + c]).then_inc(lru_tanh, 1)
                act.wait_ge(lru_tanh, 2 * c + 2)
                for d in range(2):
                    f(lA[d], lA[d], ACT.Exp, scale=small[:, 40 + 4 * d + c:41 + 4 * d + c]).then_inc(lru_exp, 1)

            def lru_scale(c):
                for d in range(2):
                    act.wait_ge(lru_var, 2 * c + d + 1)
                    f(lT[d], lT[d], ACT.Sqrt).then_inc(lru_root, 1)

            def p_exponent(u):
                h = u // 2
                act.wait_ge(sc_bias, u + 1)
                f(s_sb[u % 2], s_sb[u % 2], ACT.Exp, bias=small[:, 64 + u:65 + u], scale=HD ** -0.5,
                  accum_out=small[:, 80 + u:81 + u]).then_inc(p_exp, 1)
                f(small[:, 96 + u:97 + u], par_("sink", h, h + 1), ACT.Exp, bias=small[:, 64 + u:65 + u]).then_inc(p_exp, 1)

            def pt_copy(u):
                h, qt = u // 2, u % 2
                act.wait_ge(pt_mm, u + 1)
                if h >= 2:
                    act.wait_ge(pv_mm, h - 1)
                f(p_t[h % 2][:, :, qt * P:(qt + 1) * P], PS[:, 4, :].rearrange("p (k q) -> p k q", k=4),
                  ACT.Copy).then_inc(pt_copied, 1)

            def weave_mixers(slot):
                if slot in LRU_SLOTS:
                    lru(LRU_SLOTS.index(slot))
                if slot - 1 in LRU_SLOTS:
                    lru_scale(LRU_SLOTS.index(slot - 1))
                if slot == Y_SLOT:
                    act.wait_ge(nar_dve, START + 3)
                    act.wait_ge(nar_act, START + 3)
                    f(proj[:, 8:12, :], proj[:, 8:12, :], ACT.Gelu_apprx_tanh).then_inc(gelu_ready, 1)
                u = slot - SCORE_SLOT
                if 1 <= u <= 16:
                    pt_copy(u - 1)
                if 0 <= u < 16:
                    p_exponent(u)

            for i in range(6):
                for q in range(4):
                    if q < 3:
                        early_split(4 * i + q + 2)
                    weave_mixers(5 * i + q)
                act.wait_ge(ring_out, used(T_NAR + i, 4))
                f(proj[:, 4 * i + 2:4 * i + 4, :], PS[:, 1, :].rearrange("p (s t) -> p s t", s=2), ACT.Copy).then_inc(nar_act, 1)
                early_split(4 * i + 5)
                ada_copy(A_NAR + i, T_NAR + i, 8)
                weave_mixers(5 * i + 4)

            def tokens_back(o):
                for nt in range(2):
                    act.wait_ge(hy_tmm, 2 * o + nt + 1)
                    f(ztok[:, nt, :], PS[:, 4 + nt, :], ACT.Copy).then_inc(hy_tcopied, 1)

            def gate(n, j, bank):
                act.wait_ge(ring_out, used(n * 3 + (T_MERGE + j // 2), 4 + 4 * (j % 2)))
                f(gates[j], PS[:, bank:bank + 2, :].rearrange("p a b -> p (a b)"), ACT.Sigmoid).then_inc(gate_sig, 1)

            def split(first, turn0, i):
                turn, slot, free = split_waits(i)
                act.wait_ge(ring_in[slot], (turn0 + (turn + 1)) * 16)
                act.wait_ge(ring_out, turn0 * RING + free)
                f(w_hi[i % 2], ring[:, slot], ACT.Copy).then_inc(split_hi, 1)

            def split_operand(to, x):
                f(to, x, ACT.Copy).then_inc(operand_hi, 1)

            act.wait_ge(pv_mm, 8)
            for i in range(12):
                if i < 10:
                    early_split(24 + i + 2)
                if i in (HYENA_SLOTS[0], HYENA_SLOTS[3]):
                    tokens_back(HYENA_SLOTS.index(i) // 3)
                if i == 10:
                    act.wait_ge(mix_done, 1)
                    split_operand(mix_hi, proj[:, 0:12, :])
                    split_operand(hv_hi, hv)
                if i % 4 == 3:
                    gate(0, i // 4, 0)
            split(0, T_MERGE, 12)
            split(0, T_MERGE, 13)
            ada_copy(A_MERGE, T_MERGE + 1, 8)
            for i in (14, 15):
                split(0, T_MERGE, i)
            for i in range(2):
                split(0, T_MERGE + 3, i)
            ada_copy(A_MERGE + 1, T_MERGE + 2, 8)
            with act.Fori(1, 4) as n:
                turn0 = n * 3 + T_MERGE
                for i in range(2, 16):
                    split(n, turn0, i)
                    if i < 13 and i % 4 == 0:
                        act.wait_ge(br_used, n * 3 + (START - 3 + i // 4))
                        gate(n, i // 4 - 1, 2 * (i // 4 - 1))
                    if i == 13:
                        ada_copy(n * 2 + A_MERGE, n * 3 + (T_MERGE + 1), 8)
                for i in range(2):
                    split(n, turn0 + 3, i)
                ada_copy(n * 2 + (A_MERGE + 1), n * 3 + (T_MERGE + 2), 8)
            for q in range(4):
                if q == 3:
                    act.wait_ge(merged, 4)
                split_operand(m_hi[:, 4 * q:4 * q + 4, :], m_t[:, 4 * q:4 * q + 4, :])
            act.dma_start(x_res.rearrange("p k t -> p (k t)"), x_t).then_inc(in_res, 16)
            for i in range(2, 16):
                slot = i % RING
                act.wait_ge(ring_in[slot], (T_OUT + 1 + i // RING) * 16)
                act.wait_ge(ring_out, T_OUT * RING + i - 1)
                f(w_hi[i % 2], ring[:, slot], ACT.Copy).then_inc(split_hi, 1)
            act.wait_ge(norm2_mm, 1)
            f(rbn, PS[:, 5, 0:T], ACT.Sqrt, bias=con_("eps"), scale=1.0 / D).then_inc(norm2_root, 1)
            for kt in range(KT):
                act.wait_ge(fl_scaled, kt + 1)
                f(fl[:, kt, :], fl[:, kt, :], ACT.Identity, bias=mod[:, 3 * KT + kt, 0:1]).then_inc(fl_ready, 1)

            def tokens_copy(w):
                q, tt = w // 2, w % 2
                act.wait_ge(ft_mm, w + 1)
                f(fl_tok[:, tt, q * 512:(q + 1) * 512], PS[:, w % 4, :], ACT.Copy).then_inc(ft_copied, 1)

            act.wait_ge(router_mm, 1)
            f(rlog, PS[0:EXPERTS, 4, 0:T], ACT.Copy).then_inc(router_sb, 1)
            for w in range(2):
                tokens_copy(w)
            act.wait_ge(router_arg, 1)
            f(rt[:, 96:128], rt[:, 64:96], ACT.Exp).then_inc(router_exp, 1)
            for w in range(2, 8):
                tokens_copy(w)
            act.wait_ge(route_ready, 1)
            nr = act.value_load(rounds_i[0:1, 0:1], min_val=1, max_val=MAX_ROUNDS)

            def group(it):
                for p in range(2):
                    pair = it * 2 + p
                    c0 = it * (2 * PAIR_CHUNKS) + PAIR_CHUNKS * p
                    act.wait_ge(moe_out, c0 + 8)
                    act.wait_ge(act_ready, START + pair)
                    f(sg, PS[:, 0, :], ACT.Silu).then_inc(silu_done, 1)
                    act.wait_ge(at_mm, START + pair + 1)
                    f(act_t.rearrange("p k s -> p (k s)"), PS[:, 2, :], ACT.Copy).then_inc(at_copied, 1)
                    act.wait_ge(acc_mm, START + it * 24 + (8 + 12 * p))
                    for n in range(4):
                        act.wait_ge(moe_out, c0 + (16 + 2 * n + 2))
                        f(yg[:, n * 512:(n + 1) * 512], PS[:, 4 + n % 2, :], ACT.Copy).then_inc(dn_copied, 1)

            with act.Fori(0, nr) as r:
                with act.Fori(0, 4) as g:
                    group(r * 4 + g)
            act.wait_ge(y_ready, 1)
            for kt in range(0, KT, 2):
                f(squares[:, kt, :], x_res[:, kt, :], ACT.Square).then_inc(sq3_ready, 1)
            act.wait_ge(norm3_mm, 1)
            f(rbn, PS[:, 5, 0:T], ACT.Sqrt, bias=con_("eps"), scale=1.0 / D).then_inc(norm3_root, 1)

        @block.gpsimd
        def _(pool):
            for n in range(44):
                slot = n % 4 if n < 32 else (n - 32) % RING
                buffers = wide_hi if n < 8 else early_hi[n >= 16]
                pool.wait_ge(early_split_hi, n + 1)
                for k in (0, 2):
                    pool.tensor_tensor(ring_r[:, slot, k:k + 2], ring[:, slot, k:k + 2], buffers[n % 2][:, k:k + 2],
                                       ALU.subtract).then_inc(early_split_lo, 1)

        @block.vector
        def _(dve):
            for begun in (ada_added, nar_dve, br_used, out_used, acc_done, act_ready, ct_copied):
                dve.sem_inc(begun, START)
            step = Steps(dve, dve_main)

            dve.memset(silu_c[:, :, :], 0.0).then_inc(silu_zero, 1)
            dve.wait_ge(in_par, 16)
            def ada_add(a):
                dve.wait_ge(ada_turned, START + a + 1)
                lo = PARAM_AT["b_ada"][0]
                sums = PS[:, 7, :].rearrange("p (c j r) -> p c r j", c=4, j=4)[:, :, 0:2, :]
                dve.tensor_reduce(ada_sum.rearrange("p (c r) -> p c r", c=4), sums, AX.X, ALU.add).then_inc(ada_summed, 1)
                dve.wait_ge(ada_summed, a + 1)
                dve.tensor_tensor(mod[:, bass.ds(a * 4, 4), :].rearrange("p k b -> p (k b)"), ada_sum,
                                  par[:, bass.ds(a * 8 + lo, 8)], ALU.add).then_inc(ada_added, 1)

            def stream_squares():
                dve.wait_ge(in_con, 16)
                dve.wait_ge(in_x, 16)
                dve.wait_ge(in_ctx, 16)
                for kt in range(KT):
                    if kt >= 2:
                        dve.wait_ge(norm_mm, kt - 1)
                    dve.tensor_tensor(sq[:, kt % 2].rearrange("p (s t) -> p s t", s=2), norm_x[:, :, kt, :],
                                      norm_x[:, :, kt, :], ALU.mult).then_inc(sq_ready, 1)

            def reduced(i, bank, bias):
                a, k = fa[0:64, :], fk[0:64, :]
                dve.wait_ge(arg_mm, i + 1)
                if i:
                    dve.wait_ge(sin_ready, i)
                step.done(dve.tensor_scalar(a, PS[0:64, bank, 0:T], par_(bias)[0:64], par_("freq")[0:64], ALU.add, ALU.mult))
                step.done(dve.tensor_scalar(k, a, 1.0 / TWO_PI, ROUND_MAGIC, ALU.mult, ALU.add))
                step.done(dve.tensor_scalar(k, k, -ROUND_MAGIC, None, ALU.add))
                for part in TWO_PI_PARTS:
                    step.done(dve.scalar_tensor_tensor(out=a, in0=k, scalar=-part, in1=a, op0=ALU.mult, op1=ALU.add))
                dve.tensor_scalar(a, a, 3.1415925, -3.1415925, ALU.min, ALU.max).then_inc(arg_ready, 1)

            def normalise_streams():
                for kt in range(KT):
                    for s in range(2):
                        last = dve.tensor_tensor(norm_x[:, s, kt, :], norm_x[:, s, kt, :], rbc[:, s * T:(s + 1) * T], ALU.mult)
                last.then_inc(norm_ready, 1)

            def filter_windowed(o):
                if o == 0:
                    dve.wait_ge(in_win, 16)
                for u in range(4):
                    nt, d = u // 2, u % 2
                    dve.wait_ge(tap_mm, 4 * o + u + 1)
                    last = dve.tensor_tensor(taps[:, nt, d, :], PS[:, u, :], win[:, d, nt, :], ALU.mult)
                step.done(last)
                dve.tensor_tensor(tsq[:, :, :, :], taps[:, :, :, :], taps[:, :, :, :], ALU.mult)
                if o:
                    dve.wait_ge(spec_mm, 4)
                step.done(dve.tensor_tensor(tapsum[:, :, 0, :], taps[:, :, 0, :], taps[:, :, 1, :], ALU.add))
                step.done(dve.tensor_tensor(tsum[:, o, :], tsq[:, 0, 0, :], tsq[:, 0, 1, :], ALU.add))
                step.done(dve.tensor_tensor(tsum[:, o, :], tsum[:, o, :], tsq[:, 1, 0, :], ALU.add))
                step.done(dve.tensor_tensor(tsum[:, o, :], tsum[:, o, :], tsq[:, 1, 1, :], ALU.add))
                dve.tensor_tensor(tapsum[:, :, 1, :], taps[:, :, 0, :], taps[:, :, 1, :], ALU.subtract).then_inc(tapsum_ready, 1)

            z, az, u_, s_, s2, pol, c8, nc8 = (small[:, a:a + 8] for a in (112, 16, 24, 120, 128, 136, 32, 40))
            step.done(dve.tensor_scalar(z, par_("lam"), -1.0, None, ALU.mult))
            step.done(dve.tensor_tensor(az, par_("lam"), z, ALU.max))
            dve.tensor_scalar(small[:, 56:64], par_("sink"), -1.0, None, ALU.mult).then_inc(lam_exp, 1)

            for a in range(ADA_FIRST):
                ada_add(a)
                if a == 0:
                    stream_squares()
                    dve.wait_ge(norm_root, 1)
                    step.done(dve.reciprocal(rbc, rbc))
                if a == 1:
                    reduced(0, 4, "fb1")
                    normalise_streams()
                if a == 2:
                    reduced(1, 3, "fb2")
                if a in (3, 5):
                    filter_windowed((a - 3) // 2)
                if a == 6:
                    dve.wait_ge(tnorm_root, 1)
                    step.done(dve.reciprocal(small[:, 8:16], small[:, 0:8]))
            dve.wait_ge(ada_added, START + ADA_FIRST)
            dve.wait_ge(norm_ready, 1)

            def scale_gain(first, gain, cols):
                step.done(dve.tensor_scalar(modA[:, :, 0:cols], mod[:, first:first + KT, 0:cols], 1.0, None, ALU.add))
                g = par_(gain).rearrange("p (k b) -> p k b", b=2 if cols == 2 else 1)
                step.done(dve.tensor_tensor(modA[:, :, 0:cols], modA[:, :, 0:cols], g, ALU.mult))

            def both_split(kt):
                dve.wait_ge(both_high, kt + 1)
                dve.tensor_tensor(norm_r[:, :, kt, :], norm_x[:, :, kt, :], both_hi[kt // 8][:, kt % 8], ALU.subtract).then_inc(both_low, 1)

            scale_gain(KT, "g_mix", 2)
            for kt in range(KT):
                for s, b in ((0, 1), (1, 0)):
                    last = dve.tensor_scalar(norm_x[:, s, kt, :], norm_x[:, s, kt, :], modA[:, kt, b:b + 1],
                                             mod[:, kt, b:b + 1], ALU.mult, ALU.add)
                last.then_inc(h_ready, 1)
                if kt:
                    both_split(kt - 1)
            both_split(KT - 1)
            dve.wait_ge(lam_exp, 2)
            step.done(dve.tensor_scalar(s_, u_, 2.0, None, ALU.add))
            step.done(dve.reciprocal(s_, s_))
            step.done(dve.tensor_tensor(s_, s_, u_, ALU.mult))
            step.done(dve.tensor_tensor(s2, s_, s_, ALU.mult))
            step.done(dve.tensor_scalar(pol, s2, 1.0 / 19, 1.0 / 17, ALU.mult, ALU.add))
            for k in range(7, -1, -1):
                step.done(dve.tensor_tensor(pol, pol, s2, ALU.mult))
                step.done(dve.tensor_scalar(pol, pol, 1.0 / (2 * k + 1), None, ALU.add))
            step.done(dve.tensor_tensor(pol, pol, s_, ALU.mult))
            step.done(dve.tensor_scalar(z, z, 0.0, None, ALU.max))
            step.done(dve.scalar_tensor_tensor(out=z, in0=pol, scalar=2.0, in1=z, op0=ALU.mult, op1=ALU.add))
            dve.tensor_scalar(c8, z, 8.0, None, ALU.mult).then_inc(lam_ready, 1)
            step.done(dve.tensor_scalar(nc8, z, -8.0, None, ALU.mult))
            for i in range(2):
                dve.wait_ge(ring_out, used(T_WIDE + i, 4))
                for c in (0, 2):
                    dve.tensor_copy(kvx[:, 4 * i + c, :, :], PS[:, c, :].rearrange("p (s t) -> p s t", s=2)).then_inc(kv_dve, 1)
                ada_add(ADA_FIRST + i)
            dve.wait_ge(latent_hi, 4)
            dve.wait_ge(in_late, 16)
            dve.wait_ge(kv_dve, 4)
            dve.wait_ge(kv_act, 4)
            for c in range(CT):
                x, y = kvx[:, 4 + c, :, :], xc[:, c, :].rearrange("p (s t) -> p s t", s=2)
                w = lambda j: par_("lru_w", 4 * j + c, 4 * j + c + 1)
                step.done(dve.tensor_scalar(y, x, w(2), par_("lru_b", c, c + 1), ALU.mult, ALU.add))
                step.done(dve.scalar_tensor_tensor(out=y[:, :, 2:T], in0=x[:, :, 0:T - 2], scalar=w(0), in1=y[:, :, 2:T], op0=ALU.mult, op1=ALU.add))
                step.done(dve.scalar_tensor_tensor(out=y[:, :, 1:T], in0=x[:, :, 0:T - 1], scalar=w(1), in1=y[:, :, 1:T], op0=ALU.mult, op1=ALU.add))
                dve.scalar_tensor_tensor(out=y[:, :, 0:T - 1], in0=x[:, :, 1:T], scalar=w(3), in1=y[:, :, 0:T - 1], op0=ALU.mult, op1=ALU.add).then_inc(lru_in, 1)

            def lru(c):
                if c == 0:
                    dve.wait_ge(lru_in, CT)
                for d in range(2):
                    dve.wait_ge(lru_exp, 2 * c + d + 1)
                    dve.tensor_tensor(lB[d], lB[d], xc[:, c, :], ALU.mult)
                    step.done(dve.tensor_tensor(lU, lA[d], lA[d], ALU.mult))
                    dve.scalar_tensor_tensor(out=lT[d], in0=lU, scalar=1.0, in1=lT[d], op0=ALU.add, op1=ALU.mult).then_inc(lru_var, 1)
                    dve.wait_ge(lru_var, 2 * c + d + 1)

            def lru_scan(c):
                for d in range(2):
                    dve.wait_ge(lru_root, 2 * c + d + 1)
                    step.done(dve.tensor_tensor(lB[d], lB[d], lT[d], ALU.mult))
                    if d == 0:
                        step.done(dve.tensor_tensor_scan(lT[0], lA[0], lB[0], 0.0, ALU.mult, ALU.add))
                    else:
                        for s in range(2):
                            o_, a_, b_ = (t[:, s * T:(s + 1) * T][:, ::-1] for t in (lT[1], lA[1], lB[1]))
                            step.done(dve.tensor_tensor_scan(o_, a_, b_, 0.0 if s == 0 else lT[1][:, 0:1], ALU.mult, ALU.add))
                dve.tensor_tensor(xc[:, c, 0:T], lT[0][:, T:2 * T], lT[1][:, T:2 * T], ALU.add).then_inc(lru_in, 1)
                dve.wait_ge(lru_in, CT + c + 1)

            def rotate(u):
                dve.wait_ge(rot_mm, u + 1)
                src = kvx[:, 0:2, 1, :] if u == 0 else proj[:, 2 * u - 2:2 * u, :]
                for h in range(2):
                    dve.tensor_tensor(rtmp[:, h * T:(h + 1) * T], PS[:, 4 + u % 2, h * T:(h + 1) * T], rope[:, 1, :], ALU.mult)
                    last = dve.tensor_tensor(src[:, h, :], src[:, h, :], rope[:, 0, :], ALU.mult)
                step.done(last)
                last = dve.tensor_tensor(src, src, rtmp.rearrange("p (s t) -> p s t", s=2), ALU.add)
                last.then_inc(rot_used, 1)
                dve.wait_ge(rot_used, u + 1)

            def row_max(u):
                h, qt = u // 2, u % 2
                dve.wait_ge(sc_mm, u + 1)
                if u >= 2:
                    dve.wait_ge(pt_mm, u - 1)
                dve.tensor_tensor_reduce(s_sb[u % 2], PS[:, 2 + u % 2, :], mask[:, qt, :], 1.0, NEG, ALU.add, ALU.max,
                                         small[:, 144 + u:145 + u]).then_inc(sc_read, 1)
                dve.wait_ge(sc_read, u + 1)
                dve.tensor_scalar(small[:, 64 + u:65 + u], small[:, 144 + u:145 + u], -(HD ** -0.5), small[:, 56 + h:57 + h],
                                  ALU.mult, ALU.min).then_inc(sc_bias, 1)

            def normalise(u):
                dve.wait_ge(p_exp, 2 * u + 2)
                den = small[:, 160 + u:161 + u]
                step.done(dve.tensor_tensor(den, small[:, 80 + u:81 + u], small[:, 96 + u:97 + u], ALU.add))
                step.done(dve.reciprocal(den, den))
                dve.tensor_scalar(s_sb[u % 2], s_sb[u % 2], den, None, ALU.mult).then_inc(p_ready, 1)

            def pv_copy(h):
                dve.wait_ge(pv_mm, h + 1)
                dve.tensor_copy(proj[:, h, :], PS[:, 5, 0:T]).then_inc(pv_copied, 1)

            def short_conv(src, dst, wi):
                w = lambda j: par_("hy_w", 12 * j + wi, 12 * j + wi + 1)
                step.done(dve.tensor_scalar(dst, src, w(1), par_("hy_b", wi, wi + 1), ALU.mult, ALU.add))
                step.done(dve.scalar_tensor_tensor(out=dst[:, 1:T], in0=src[:, 0:T - 1], scalar=w(0), in1=dst[:, 1:T], op0=ALU.mult, op1=ALU.add))
                return dve.scalar_tensor_tensor(out=dst[:, 0:T - 1], in0=src[:, 1:T], scalar=w(2), in1=dst[:, 0:T - 1], op0=ALU.mult, op1=ALU.add)

            def projected(panels):
                dve.wait_ge(nar_dve, START + panels)
                dve.wait_ge(nar_act, START + panels)

            def weave_mixers(slot):
                if slot in LRU_SLOTS:
                    lru(LRU_SLOTS.index(slot))
                if slot - 1 in LRU_SLOTS:
                    lru_scan(LRU_SLOTS.index(slot - 1))
                for u in ROTATE_SLOTS.get(slot, ()):
                    rotate(u)
                if slot == VALUE_SLOT:
                    dve.wait_ge(vt_mm, 1)
                    dve.tensor_copy(v_tok.rearrange("p k c -> p (k c)"), PS[:, 4:6, :].rearrange("p a b -> p (a b)")).then_inc(vt_copied, 1)
                u = slot - SCORE_SLOT
                if 0 <= u < 16:
                    row_max(u)
                if u >= 3 and u % 2 == 1 and u <= 17:
                    pv_copy((u - 3) // 2)
                if 0 <= u < 16:
                    normalise(u)
                if slot == Y_SLOT + 1:
                    dve.wait_ge(gelu_ready, 1)
                    last = dve.tensor_tensor(proj[:, 8:12, :], proj[:, 8:12, :], xc[:, :, 0:T], ALU.mult)
                    last.then_inc(lru_done, 1)
                    dve.wait_ge(lru_done, 1)
                if 20 <= slot < 24:
                    projected(4)
                    c = slot - 20
                    ins = short_conv(proj[:, 12 + c, :], hv[:, c, :], c)
                    if c < 3:
                        step.done(ins)
                    else:
                        ins.then_inc(hy_in, 1)
                        dve.wait_ge(hy_in, 1)
                if 25 <= slot < 29:
                    projected(5)
                    c = slot - 25
                    step.done(short_conv(proj[:, 16 + c, :], proj[:, 12 + c, :], 4 + c))

            for i in range(6):
                for q in range(4):
                    weave_mixers(5 * i + q)
                dve.wait_ge(ring_out, used(T_NAR + i, 4))
                dve.tensor_copy(proj[:, 4 * i:4 * i + 2, :], PS[:, 0, :].rearrange("p (s t) -> p s t", s=2)).then_inc(nar_dve, 1)
                ada_add(A_NAR + i)
                weave_mixers(5 * i + 4)
            projected(6)
            for c in range(CT):
                step.done(short_conv(proj[:, 20 + c, :], proj[:, 16 + c, :], 8 + c))

            for o in range(2):
                for kk in range(2):
                    dve.wait_ge(hy_fmm, 4 * o + 2 * kk + 2)
                    zr, zs = PS[:, 2 + 2 * kk, :], PS[:, 3 + 2 * kk, :]
                    hr, hs = spec[:, kk, o, :], spec[:, 2 + kk, o, :]
                    dve.tensor_tensor(ht[0], zr, hr, ALU.mult)
                    step.done(dve.tensor_tensor(ht[1], zs, hs, ALU.mult))
                    step.done(dve.tensor_tensor(ysp[:, kk, :], ht[0], ht[1], ALU.subtract))
                    dve.tensor_tensor(ht[0], zr, hs, ALU.mult)
                    step.done(dve.tensor_tensor(ht[1], zs, hr, ALU.mult))
                    last = dve.tensor_tensor(ysp[:, 2 + kk, :], ht[0], ht[1], ALU.add)
                    if kk == 0:
                        step.done(last)
                last.then_inc(hy_ready, 1)
                for c in range(CT):
                    dve.wait_ge(hy_imm, 4 * o + 2 * (c // 2) + 2)
                    z = hv[:, c, :]
                    t = ht[c % 2][:, 0:T]
                    step.done(dve.tensor_scalar(t, PS[:, 2 + c // 2, (c % 2) * T:(c % 2 + 1) * T], small[:, 8 + 4 * o + c:9 + 4 * o + c], None, ALU.mult))
                    step.done(dve.scalar_tensor_tensor(out=z, in0=z, scalar=par_("skip", 4 * o + c, 4 * o + c + 1), in1=t, op0=ALU.mult, op1=ALU.add))
                    ins = dve.tensor_tensor(z, z, proj[:, 12 + 4 * o + c, :], ALU.mult)
                    if c < 3:
                        step.done(ins)
                    elif o == 0:
                        ins.then_inc(hy_in, 1)
                        dve.wait_ge(hy_in, 2)
                    else:
                        ins.then_inc(mix_done, 1)

            def split(count, i, slot):
                dve.wait_ge(split_hi, count + 1)
                dve.tensor_tensor(ring_r[:, slot], ring[:, slot], w_hi[i % 2], ALU.subtract).then_inc(split_lo, 1)

            def split_operand(count, low, x, high):
                dve.wait_ge(operand_hi, count)
                dve.tensor_tensor(low, x, high, ALU.subtract).then_inc(operand_lo, 1)

            def merge(n, j):
                m = m_t[:, bass.ds(n * 4, 4), :].rearrange("p k t -> p (k t)")
                dve.wait_ge(gate_sig, n * 3 + (j + 1))
                dve.wait_ge(ring_out, used(n * 3 + (T_MERGE + 2), 2 + j))
                src = PS[:, 2 * j:2 * j + 2, :].rearrange("p a b -> p (a b)")
                dve.tensor_tensor(m if j == 0 else gtmp, src, gates[j], ALU.mult).then_inc(br_used, 1)
                dve.wait_ge(br_used, START + n * 3 + (j + 1))
                if j:
                    ins = dve.tensor_tensor(m, m, gtmp, ALU.add)
                    if j == 1:
                        ins.then_inc(summed, 1)
                        dve.wait_ge(summed, n + 1)
                    else:
                        ins.then_inc(merged, 1)
                        dve.wait_ge(merged, n + 1)

            split_operand(1, mix_lo, proj[:, 0:12, :], mix_hi)
            split_operand(2, hv_lo, hv, hv_hi)
            split(0, 0, 0)
            split(1, 1, 1)
            ada_add(A_MERGE)
            split(2, 2, 2)
            split(3, 3, 3)
            merge(0, 0)
            split(4, 0, 0)
            merge(0, 1)
            split(5, 1, 1)
            merge(0, 2)
            ada_add(A_MERGE + 1)
            with dve.Fori(1, 4) as n:
                first = n * 16 - 12
                for i in range(2, 16):
                    split(first + i, i, split_waits(i)[1])
                    if i == 13:
                        ada_add(n * 2 + A_MERGE)
                merge(n, 0)
                split(first + 16, 0, 0)
                merge(n, 1)
                split(first + 17, 1, 1)
                merge(n, 2)
                ada_add(n * 2 + (A_MERGE + 1))
            for q in range(4):
                split_operand(3 + q, *(b[:, 4 * q:4 * q + 4, :] for b in (m_lo, m_t, m_hi)))

            dve.wait_ge(ada_added, START + ADA_PANELS)
            for p in range(4):
                for i in range(4 * p + 2, min(4 * p + 5, 16)):
                    split(52 + i, i, i % RING)
                if p == 0:
                    step.done(dve.memset(sqsum, 0.0))
                    dve.wait_ge(in_res, 16)
                dve.wait_ge(ring_out, used(T_OUT, 4 * p + 4))
                for c in range(4):
                    kt = 4 * p + c
                    x = x_res[:, kt, :]
                    if c == 2 and p < 3:
                        split(52 + 4 * p + 5, 1, (4 * p + 5) % RING)
                    ins = dve.scalar_tensor_tensor(out=x, in0=PS[:, 2 * (p % 2) + c // 2, (c % 2) * T:(c % 2 + 1) * T],
                                                   scalar=mod[:, 2 * KT + kt, 0:1], in1=x, op0=ALU.mult, op1=ALU.add)
                    step.done(ins)
                    if c == 3:
                        dve.tensor_copy(small[:, 176:177], small[:, 8:9]).then_inc(out_used, 1)
                    step.done(dve.tensor_tensor(sqn, x, x, ALU.mult))
                    step.done(dve.tensor_tensor(sqsum, sqsum, sqn, ALU.add))
            dve.wait_ge(out_used, START + 4)
            dve.tensor_copy(small[:, 177:178], small[:, 8:9]).then_inc(sq2_ready, 1)
            step.done(dve.tensor_scalar(modA[:, :, 0], mod[:, 4 * KT:5 * KT, 0], 1.0, None, ALU.add))
            step.done(dve.tensor_tensor(modA[:, :, 0], modA[:, :, 0], par_("g_ffn"), ALU.mult))
            dve.wait_ge(norm2_root, 1)
            step.done(dve.reciprocal(rbn, rbn))
            for kt in range(KT):
                dve.scalar_tensor_tensor(out=fl[:, kt, :], in0=x_res[:, kt, :], scalar=modA[:, kt, 0:1], in1=rbn,
                                         op0=ALU.mult, op1=ALU.mult).then_inc(fl_scaled, 1)

            t3 = lambda a, n=16: rt[:, a:a + 2 * n].rearrange("p (t e) -> p t e", t=2)
            logit, shifted, prob, pick1, pick2, tmp, eq = (t3(32 * k) for k in range(1, 8))
            gm, gq = t3(288, 4), t3(296, 4)
            col = lambda k: small[:, 180 + 2 * k:182 + 2 * k]
            dve.wait_ge(router_turned, 1)
            for tt in range(2):
                last = dve.tensor_tensor(logit[:, tt, :], PS[:, 5, 64 + tt * 16:80 + tt * 16], par_("router_b"), ALU.add)
            step.done(last)
            step.done(dve.tensor_reduce(col(0), logit, AX.X, ALU.max))
            for tt in range(2):
                last = dve.tensor_scalar(shifted[:, tt, :], logit[:, tt, :], col(0)[:, tt:tt + 1], None, ALU.subtract)
            last.then_inc(router_arg, 1)
            dve.wait_ge(router_exp, 1)
            step.done(dve.tensor_reduce(col(1), prob, AX.X, ALU.add))
            step.done(dve.reciprocal(col(1), col(1)))
            for tt in range(2):
                last = dve.tensor_scalar(prob[:, tt, :], prob[:, tt, :], col(1)[:, tt:tt + 1], None, ALU.mult)
            step.done(last)

            def first_max(values, out_, scratch, down, top):
                step.done(dve.tensor_reduce(top, values, AX.X, ALU.max))
                for tt in range(2):
                    last = dve.scalar_tensor_tensor(out=scratch[:, tt, :], in0=values[:, tt, :], scalar=top[:, tt:tt + 1],
                                                    in1=down, op0=ALU.is_equal, op1=ALU.mult)
                step.done(last)
                step.done(dve.tensor_reduce(col(7), scratch, AX.X, ALU.max))
                for tt in range(2):
                    last = dve.tensor_scalar(out_[:, tt, :], scratch[:, tt, :], col(7)[:, tt:tt + 1], None, ALU.is_equal)
                step.done(last)

            step.done(dve.tensor_reduce(gm.rearrange("p t g -> p (t g)"), rt[:, 96:128].rearrange("p (g e) -> p g e", e=4), AX.X, ALU.max))
            first_max(gm, gq, t3(304, 4), con_("down4"), col(2))
            for g in range(8):
                a = g * 4
                last = dve.tensor_scalar(rt[:, 192 + a:196 + a], rt[:, 96 + a:100 + a], rt[:, 296 + g:297 + g], None, ALU.mult)
            step.done(last)
            step.done(dve.tensor_scalar(rt[:, 296:304], rt[:, 296:304], -1.0, None, ALU.add))
            for g in range(8):
                a = g * 4
                last = dve.tensor_scalar(rt[:, 192 + a:196 + a], rt[:, 192 + a:196 + a], rt[:, 296 + g:297 + g], None, ALU.add)
            step.done(last)
            first_max(tmp, pick1, eq, con_("down16"), col(3))
            step.done(dve.scalar_tensor_tensor(out=rt[:, 192:224], in0=rt[:, 128:160], scalar=-4.0, in1=rt[:, 192:224], op0=ALU.mult, op1=ALU.add))
            first_max(tmp, pick2, eq, con_("down16"), col(4))
            dve.tensor_tensor(rt[:, 0:32], rt[:, 128:160], rt[:, 160:192], ALU.add).then_inc(pick_ready, 1)
            step.done(dve.tensor_tensor(col(5), col(3), col(4), ALU.add))
            step.done(dve.reciprocal(col(5), col(5)))
            for tt in range(2):
                dve.tensor_scalar(pick1[:, tt, :], pick1[:, tt, :], col(3)[:, tt:tt + 1], col(5)[:, tt:tt + 1], ALU.mult, ALU.mult)
                last = dve.tensor_scalar(pick2[:, tt, :], pick2[:, tt, :], col(4)[:, tt:tt + 1], col(5)[:, tt:tt + 1], ALU.mult, ALU.mult)
            step.done(last)
            step.done(dve.tensor_tensor(weight, rt[:, 128:160], rt[:, 160:192], ALU.add))
            dve.wait_ge(rank_mm, 1)
            dve.wait_ge(pick_ready, 1)
            step.done(dve.scalar_tensor_tensor(out=rank, in0=PS[:, 5, 0:32], scalar=1.0, in1=rt[:, 0:32], op0=ALU.add, op1=ALU.mult))
            step.done(dve.tensor_scalar(rank, rank, -1.0, None, ALU.add))
            step.done(dve.tensor_reduce(small[:, 200:201], PS[:, 5, 32:48], AX.X, ALU.max))
            for k in range(1, MAX_ROUNDS):
                step.done(dve.tensor_scalar(small[:, 200 + k:201 + k], small[:, 200:201], float(k * SLOTS), None, ALU.is_gt))
            step.done(dve.memset(small[:, 200:201], 1.0))
            step.done(dve.tensor_reduce(small[:, 204:205], small[:, 200:204], AX.X, ALU.add))
            dve.tensor_copy(rounds_i[:, :], small[0:1, 204:205]).then_inc(route_ready, 1)
            dve.wait_ge(route_ready, 1)
            nr = dve.value_load(rounds_i[0:1, 0:1], min_val=1, max_val=MAX_ROUNDS)

            def dispatch(g):
                for tt in range(2):
                    for e in range(4):
                        r_ = rank[:, bass.ds(g * 4 + (16 * tt + e), 1)]
                        last = dve.tensor_scalar(disp[:, tt, e * SLOTS:(e + 1) * SLOTS], con_("iota"), r_, None, ALU.is_equal)
                last.then_inc(disp_ready, 1)

            def gathered(turn, to, v):
                dve.wait_ge(acc_mm, turn + (START + 1))
                dve.tensor_copy(xg[to][:, 2 * v:2 * v + 2, :], PS[:, 6 + v % 2, :].rearrange("p (f t) -> p f t", f=2)).then_inc(acc_done, 1)

            def group(it, g, following, now):
                for tt in range(2):
                    for e in range(4):
                        r_ = rank[:, bass.ds(g * 4 + (16 * tt + e), 1)]
                        w_ = weight[:, bass.ds(g * 4 + (16 * tt + e), 1)]
                        last = dve.tensor_scalar(comb[:, tt, e * SLOTS:(e + 1) * SLOTS], con_("iota"), r_, w_, ALU.is_equal, ALU.mult)
                last.then_inc(comb_ready, 1)
                dve.wait_ge(comb_ready, it + 1)
                for tt in range(2):
                    r_ = rank[:, bass.ds(g * 4 + 16 * tt, 4)]
                    dve.tensor_scalar(r_, r_, -float(SLOTS), None, ALU.add).then_inc(dve_moe, 1)
                dve.wait_ge(dve_moe, it * 2 + 2)
                dispatch(following)
                for p in range(2):
                    pair = it * 2 + p
                    for v_ in range(4):
                        gathered(it * 24 + (8 + 12 * p + v_), 1 - now, 4 * p + v_)
                    dve.wait_ge(ct_mm, pair + 1)
                    dve.tensor_copy(cw_t, PS[:, 3, 0:T]).then_inc(ct_copied, 1)
                    dve.wait_ge(silu_done, START + pair + 1)
                    dve.wait_ge(moe_out, it * (2 * PAIR_CHUNKS) + (PAIR_CHUNKS * p + 16))
                    dve.wait_ge(at_mm, START + pair)
                    dve.tensor_tensor(act_sb, PS[:, 1, :], sg, ALU.mult).then_inc(act_ready, 1)
                    for v_ in range(8):
                        dve.wait_ge(acc_mm, START + it * 24 + (8 + 12 * p + 4 + v_ + 1))
                        for f in range(2):
                            x = x_res[:, 2 * v_ + f, :]
                            last = dve.scalar_tensor_tensor(out=x, in0=PS[:, 6 + v_ % 2, f * T:(f + 1) * T],
                                                            scalar=mod[:, 5 * KT + 2 * v_ + f, 0:1], in1=x, op0=ALU.mult, op1=ALU.add)
                        last.then_inc(acc_done, 1)

            dispatch(0)
            for v_ in range(8):
                gathered(v_, 0, v_)
            with dve.Fori(0, nr) as r:
                with dve.Fori(0, 2) as h:
                    group(r * 4 + h * 2, h * 2, h * 2 + 1, 0)
                    group(r * 4 + h * 2 + 1, h * 2 + 1, h * -2 + 2, 1)

            end = Steps(dve, dve_end)
            dve.memset(small[:, 210:211], 0.0).then_inc(y_ready, 1)
            dve.wait_ge(y_ready, 1)
            for kt in range(1, KT, 2):
                dve.tensor_tensor(squares[:, kt, :], x_res[:, kt, :], x_res[:, kt, :], ALU.mult).then_inc(sq4_ready, 1)
            dve.wait_ge(norm3_root, 1)
            end.done(dve.reciprocal(rbn, rbn))
            for kt in range(KT):
                last = dve.scalar_tensor_tensor(out=x_res[:, kt, :], in0=x_res[:, kt, :], scalar=par_("final_g", kt, kt + 1),
                                                in1=rbn, op0=ALU.mult, op1=ALU.mult)
                if kt % 4 == 3:
                    last.then_inc(out_ready, 1)


def _constants():
    f = np.float32
    con = np.zeros((P, CONST_N), f)

    def put(name, a):
        lo, hi = CONST_AT[name]
        con[:, lo:hi] = np.broadcast_to(np.asarray(a, f).reshape(-1, hi - lo), (P, hi - lo))

    p = np.arange(P)
    put("ident", np.eye(P))
    put("ones", np.ones((P, P)))
    put("before", p[:, None] < p[None, :])
    rot = np.zeros((P, P))
    rot[p[:64] + 64, p[:64]] = -1.0
    rot[p[:64], p[:64] + 64] = 1.0
    put("rot", rot)
    put("iota", np.arange(SLOTS))
    put("eps", np.full((1, 1), EPS))
    put("down16", EXPERTS - np.arange(EXPERTS))
    put("down4", GROUPS - np.arange(GROUPS))
    tok = np.arange(T)
    inv = (f(10000.0) ** (-np.arange(32, dtype=f) / f(32))).astype(f)
    ang = np.concatenate([(tok // GRID_W).astype(f)[:, None] * inv, (tok % GRID_W).astype(f)[:, None] * inv], 1)
    ang = np.concatenate([ang, ang], 1).T
    put("rope", np.concatenate([np.cos(ang), np.sin(ang)], 1))
    mask = np.zeros((P, 2, 512))
    for qt in range(2):
        qi = qt * P + p
        mask[:, qt, T:] = np.where(np.abs(qi[:, None] - tok[None, :]) <= WINDOW, 0.0, NEG)
    put("mask", mask.reshape(P, -1))
    theta = (2.0 * np.arange(T) + 1.0) * np.pi / (2 * T)
    n = np.arange(T)
    cs = np.concatenate([np.cos(n[:, None] * theta), np.sin(n[:, None] * theta)], 1)
    put("dft", cs.reshape(2, P, 2 * T).transpose(1, 0, 2).reshape(P, -1))
    back = np.concatenate([np.cos(theta[:, None] * n), np.sin(theta[:, None] * n)], 0) / T
    put("idft", back.reshape(4, P, T).transpose(1, 0, 2).reshape(P, -1))

    t = np.linspace(0.0, 1.0, T, dtype=f)[:, None]
    w = (f(TWO_PI) * np.arange(T, dtype=f)[:, None] / f(T)).astype(f)
    bands = np.linspace(1e-4, BANDS - 1, BANDS, dtype=f)[None, :]
    z = np.concatenate([t, np.cos(bands * w), -np.sin(bands * w)], 1).T
    deltas = np.abs(np.linspace(np.log(1e-2) / 0.3, np.log(1e-2) / 1.5, HY, dtype=f))
    win = np.exp(-t * deltas[None, :]).astype(f)
    back_win = win.copy()
    back_win[0] = 0.0
    windows = np.stack([win, back_win]).reshape(2, 2, P, HY).transpose(2, 0, 1, 3).reshape(P, -1)
    return con, z.astype(f), np.ascontiguousarray(windows)


def _panels(w):
    k, n = w.shape
    return w.reshape(k // 512, 4, P, n // 512, 512).transpose(3, 0, 2, 1, 4).reshape(-1, P, CHUNK)


IN_ORDER = [0, 1, 2, 3, 7, 4, 5, 6] + list(range(8, 20))


def _cols(v):
    v = np.asarray(v)
    return v.reshape(-1, P).T


def kernel(**inputs):
    from concourse import bacc
    from concourse.bass_utils import run_bass_kernel_spmd

    a = {k: np.asarray(v) for k, v in inputs.items()}
    consts, z, windows = _constants()
    par = np.zeros((P, PARAM_N), np.float32)

    def put(name, x):
        lo, hi = PARAM_AT[name]
        par[:, lo:hi] = x

    def put64(name, x):
        lo, hi = PARAM_AT[name]
        par[:FILTER_HIDDEN, lo:hi] = x.reshape(FILTER_HIDDEN, 1)

    put("cond", np.stack([_cols(a["c"][0]), _cols(a["c_ctx"])], 2).reshape(P, -1))
    put("b_ada", np.repeat(_cols(a["b_ada"][0]), 2, axis=1))
    put("g_mix", np.repeat(_cols(a["g_mix"][0]), 2, axis=1))
    put("g_ffn", _cols(a["g_ffn"][0]))
    put("final_g", _cols(a["final_g"]))
    put("sink", np.broadcast_to(a["attn_sink"][0], (P, HEADS)))
    put("hy_w", _cols(a["hy_short_w"][0]))
    put("hy_b", _cols(a["hy_short_b"][0]))
    put("skip", _cols(a["hy_skip"][0]))
    put("lru_w", _cols(a["lru_conv_w"][0]))
    put("lru_b", _cols(a["lru_conv_b"][0]))
    put("lru_ba", _cols(a["lru_ba"][0]))
    put("lru_bx", _cols(a["lru_bx"][0]))
    put("lam", _cols(a["lru_lambda"][0]))
    put64("freq", a["hy_freq"][0])
    put64("fb1", a["hy_b1"][0])
    put64("fb2", a["hy_b2"][0])
    put("router_b", np.broadcast_to(a["router_b"], (P, EXPERTS)))
    put("router_w", a["router_w"].reshape(KT, P, EXPERTS).transpose(1, 0, 2).reshape(P, -1))

    lru_w = np.zeros((P, CT, 2, 2, P), np.float32)
    for k, name in enumerate(("lru_wa", "lru_wx")):
        for d in range(2):
            for b in range(HY // LRU_BLOCK):
                o = (b % 2) * LRU_BLOCK
                lru_w[o:o + LRU_BLOCK, b // 2, d, k, o:o + LRU_BLOCK] = a[name][0, d, b]

    filt_in = np.zeros((FILTER_HIDDEN, 384), np.float32)
    filt_in[:33, 0:T] = z
    filt_in[:33, 256:320] = a["hy_w1"][0]
    filt_in[:, 320:384] = a["hy_w2"][0]

    down = a["exp_w_down"][0].reshape(EXPERTS, 4, P, 4, 512).transpose(0, 3, 2, 1, 4).reshape(EXPERTS, 4, P, CHUNK)
    ups = [a[n][0].reshape(EXPERTS, 4, 4, P, 512).transpose(0, 1, 3, 2, 4).reshape(EXPERTS, 4, P, CHUNK)
           for n in ("exp_w_gate", "exp_w_up")]
    w_exp = np.stack([ups[0], ups[1], down])
    w_exp = w_exp.reshape(3, PAIRS, 2, 4, P, CHUNK).transpose(1, 0, 3, 2, 4, 5).reshape(-1, P, CHUNK)

    def tiles(x):
        return x.reshape(T, KT, P).transpose(2, 1, 0).reshape(P, -1)

    arrays = {
        "w_ada": _panels(a["w_ada"][0]),
        "w_in": _panels(a["w_in"][0]).reshape(20, 4, P, CHUNK)[IN_ORDER].reshape(-1, P, CHUNK),
        "w_br": _panels(np.concatenate([a["w_br_attn"][0], a["w_br_hy"][0], a["w_br_lru"][0]])),
        "w_out": _panels(a["w_out"][0]),
        "w_exp": w_exp,
        "x_t": tiles(a["x"][0]),
        "ctx_t": tiles(a["ctx"][0]),
        "params": par,
        "consts": consts,
        "lru_w": lru_w.reshape(P, -1),
        "windows": windows,
        "filt_in": filt_in,
        "filt_w": a["hy_w3"][0],
    }
    arrays = {k: np.ascontiguousarray(v) for k, v in arrays.items()}
    nc = bacc.Bacc("TRN2", target_bir_lowering=False, num_devices=1, dynamic_dma_scratch_size=1024)
    args = [nc.dram_tensor(n, v.shape, mybir.dt.from_np(v.dtype), kind="ExternalInput").ap() for n, v in arrays.items()]
    out = nc.dram_tensor("out_t", (P, KT * T), F32, kind="ExternalOutput").ap()
    build(nc, *args, out)
    r = run_bass_kernel_spmd(nc, [arrays], core_ids=[0])
    got = np.asarray(r.results[0]["out_t"])
    return got.reshape(P, KT, T).transpose(2, 1, 0).reshape(1, T, D)
```
